# Optimizing a Trainium2 kernel written in Bass

```python
import math
import jax, jax.numpy as jnp
from jax import lax
import numpy as np

D_MODEL = 1024
BATCH = 1
SEQ = 128
DEPTH = 4
DEC_BATCH = 1
DEC_SEQ = 256
PAST_LEN = 128

GRID_W = 64
N_MIXERS = 4
Q_BLOCK = 128
RMS_EPS = 1e-6
ROPE_THETA = 10000.0
NEG_INF = -1e30
D_FF = 2816
FFN_RES = 0.5
N_MOD = 9
HEAD_DIM = 64
A_HEADS = 16
A_KV_HEADS = 4
A_WINDOW = 128
B_HEADS = 16
B_KV_HEADS = 4
C_HEADS = 16
C_Q_RANK = 384
C_KV_RANK = 256
C_NOPE = 64
C_ROPE = 32
C_V = 64
C_QK = C_NOPE + C_ROPE
D_HEADS = 16
NA_ROWS = 8
NA_COLS = 16
NA_QCOLS = 16
NA_KCOLS = 2 * NA_COLS
N_A = (DEPTH + 3) // 4
N_B = (DEPTH + 2) // 4
N_C = (DEPTH + 1) // 4
N_D = DEPTH // 4

kernel_name = 'hybrid_diffusion_interleaved_step'

def rms_norm(x, g):
    xf = x.astype(jnp.float32)
    y = xf * lax.rsqrt(jnp.mean(xf * xf, axis=-1, keepdims=True) + RMS_EPS)
    return (y * g.astype(jnp.float32)).astype(x.dtype)

def modulate(x, g, shift, scale):
    return rms_norm(x, g) * (1 + scale) + shift

def modulation(cond, w, b):
    return jnp.split(jax.nn.silu(cond) @ w + b, N_MOD, axis=-1)

def half_ffn(x, shift, scale, gate, g, w_gu, w_down):
    h = modulate(x, g, shift, scale)
    a, u = jnp.split(h @ w_gu, 2, axis=-1)
    return x + FFN_RES * gate * ((jax.nn.silu(a) * u) @ w_down)

def grid_angles(n, rot_dim):
    pos = jnp.arange(n, dtype=jnp.int32)
    row = (pos // GRID_W).astype(jnp.float32)
    col = (pos % GRID_W).astype(jnp.float32)
    n_ax = rot_dim // 4
    inv = ROPE_THETA ** (-jnp.arange(n_ax, dtype=jnp.float32) / n_ax)
    return jnp.concatenate([row[:, None] * inv, col[:, None] * inv], axis=-1)

def apply_rope(x, ang):
    shape = x.shape
    xr = x.astype(jnp.float32).reshape(shape[:-1] + (shape[-1] // 2, 2))
    ang = ang.reshape(ang.shape[:1] + (1,) * (x.ndim - 3) + ang.shape[1:])
    cos, sin = jnp.cos(ang), jnp.sin(ang)
    x0, x1 = xr[..., 0], xr[..., 1]
    out = jnp.stack([x0 * cos - x1 * sin, x0 * sin + x1 * cos], axis=-1)
    return out.reshape(shape).astype(x.dtype)

def block_attention(q, k, v, sink=None):
    b, n, hkv, g, dk = q.shape
    nb = n // Q_BLOCK
    scale = dk ** -0.5
    n_keys = k.shape[1]
    qb = jnp.moveaxis(q.reshape(b, nb, Q_BLOCK, hkv, g, dk), 1, 0)

    def one_block(qi):
        s = jnp.einsum('bqhgd,bkhd->bhgqk', qi, k).astype(jnp.float32) * scale
        if sink is not None:
            s_sink = jnp.broadcast_to(sink.astype(jnp.float32).reshape(1, hkv, g, 1, 1), s.shape[:-1] + (1,))
            s = jnp.concatenate([s, s_sink], axis=-1)
        p = jax.nn.softmax(s, axis=-1)[..., :n_keys].astype(v.dtype)
        return jnp.einsum('bhgqk,bkhd->bqhgd', p, v)

    out = lax.map(one_block, qb)
    return jnp.moveaxis(out, 0, 1).reshape(b, n, hkv, g, v.shape[-1])

def window_attention(q, k, v, kc, vc, sink):
    b, n, hkv, g, d = q.shape
    nb = n // Q_BLOCK
    scale = d ** -0.5
    pad = ((0, 0), (Q_BLOCK, Q_BLOCK), (0, 0), (0, 0))
    kp = jnp.pad(k, pad).reshape(b, nb + 2, Q_BLOCK, hkv, d)
    vp = jnp.pad(v, pad).reshape(b, nb + 2, Q_BLOCK, hkv, d)
    kw = jnp.moveaxis(jnp.concatenate([kp[:, :-2], kp[:, 1:-1], kp[:, 2:]], axis=2), 1, 0)
    vw = jnp.moveaxis(jnp.concatenate([vp[:, :-2], vp[:, 1:-1], vp[:, 2:]], axis=2), 1, 0)
    qb = jnp.moveaxis(q.reshape(b, nb, Q_BLOCK, hkv, g, d), 1, 0)
    blk = jnp.arange(nb)
    qpos = blk[:, None] * Q_BLOCK + jnp.arange(Q_BLOCK)[None, :]
    kpos = (blk[:, None] - 1) * Q_BLOCK + jnp.arange(3 * Q_BLOCK)[None, :]
    valid = ((kpos[:, None, :] >= 0) & (kpos[:, None, :] < n)
             & (jnp.abs(qpos[:, :, None] - kpos[:, None, :]) <= A_WINDOW))
    sink_f = sink.astype(jnp.float32).reshape(1, hkv, g, 1, 1)
    n_win = 3 * Q_BLOCK
    n_ctx = kc.shape[1]

    def one_block(args):
        qi, ki, vi, mi = args
        s_w = jnp.einsum('bqhgd,bkhd->bhgqk', qi, ki).astype(jnp.float32) * scale
        s_w = jnp.where(mi[None, None, None], s_w, NEG_INF)
        s_c = jnp.einsum('bqhgd,bkhd->bhgqk', qi, kc).astype(jnp.float32) * scale
        s_s = jnp.broadcast_to(sink_f, s_w.shape[:-1] + (1,))
        p = jax.nn.softmax(jnp.concatenate([s_w, s_c, s_s], axis=-1), axis=-1).astype(v.dtype)
        return (jnp.einsum('bhgqk,bkhd->bqhgd', p[..., :n_win], vi)
                + jnp.einsum('bhgqk,bkhd->bqhgd', p[..., n_win:n_win + n_ctx], vc))

    out = lax.map(one_block, (qb, kw, vw, valid))
    return jnp.moveaxis(out, 0, 1).reshape(b, n, hkv, g, d)

def neighbourhood_attention(q, k, v, kc, vc, rpb):
    b, n, h, d = q.shape
    rows = n // GRID_W
    wh = min(NA_ROWS, rows)
    ncb = GRID_W // NA_QCOLS
    nqb = rows * ncb
    nk = wh * NA_KCOLS
    blk = jnp.arange(nqb)
    r = blk // ncb
    c0 = (blk % ncb) * NA_QCOLS
    rs = jnp.clip(r - wh // 2, 0, rows - wh)
    cb = jnp.clip(c0 - NA_COLS // 2, 0, GRID_W - NA_KCOLS)
    koff = jnp.arange(nk)
    kr = rs[:, None] + (koff // NA_KCOLS)[None, :]
    kcol = cb[:, None] + (koff % NA_KCOLS)[None, :]
    kidx = kr * GRID_W + kcol
    qcol = c0[:, None] + jnp.arange(NA_QCOLS)[None, :]
    cs = jnp.clip(qcol - NA_COLS // 2, 0, GRID_W - NA_COLS)
    valid = (kcol[:, None, :] >= cs[:, :, None]) & (kcol[:, None, :] < cs[:, :, None] + NA_COLS)
    ri = jnp.broadcast_to(jnp.clip(kr - r[:, None] + NA_ROWS - 1, 0, 2 * NA_ROWS - 2)[:, None, :], valid.shape)
    ci = jnp.clip(kcol[:, None, :] - qcol[:, :, None] + NA_COLS - 1, 0, 2 * NA_COLS - 2)
    scale = d ** -0.5
    qb = jnp.moveaxis(q.reshape(b, nqb, NA_QCOLS, h, d), 1, 0)
    rpb_f = rpb.astype(jnp.float32)

    def one_block(args):
        qi, idx, m, ri_i, ci_i = args
        kb = jnp.take(k, idx, axis=1)
        vb = jnp.take(v, idx, axis=1)
        s_n = jnp.einsum('bqhd,bkhd->bhqk', qi, kb).astype(jnp.float32) * scale + rpb_f[:, ri_i, ci_i][None]
        s_n = jnp.where(m[None, None], s_n, NEG_INF)
        s_c = jnp.einsum('bqhd,bkhd->bhqk', qi, kc).astype(jnp.float32) * scale
        p = jax.nn.softmax(jnp.concatenate([s_n, s_c], axis=-1), axis=-1).astype(v.dtype)
        return (jnp.einsum('bhqk,bkhd->bqhd', p[..., :nk], vb)
                + jnp.einsum('bhqk,bkhd->bqhd', p[..., nk:], vc))

    out = lax.map(one_block, (qb, kidx, valid, ri, ci))
    return jnp.moveaxis(out, 0, 1).reshape(b, n, h, d)

def gqa_project(h, w_qkv, q_norm, k_norm, n_heads, n_kv):
    b, n, _ = h.shape
    q, k, v = jnp.split(h @ w_qkv, [n_heads * HEAD_DIM, (n_heads + n_kv) * HEAD_DIM], axis=-1)
    q = rms_norm(q.reshape(b, n, n_heads, HEAD_DIM), q_norm)
    k = rms_norm(k.reshape(b, n, n_kv, HEAD_DIM), k_norm)
    return q, k, v.reshape(b, n, n_kv, HEAD_DIM)

def group_q(q, n_kv):
    b, n, hq, d = q.shape
    return q.reshape(b, n, n_kv, hq // n_kv, d)

def merge_heads(o, w_o):
    b, n = o.shape[:2]
    return o.reshape(b, n, -1) @ w_o

def mla_compress(h, w_down, q_lnorm, kv_lnorm):
    cq, ckv, kr = jnp.split(h @ w_down, [C_Q_RANK, C_Q_RANK + C_KV_RANK], axis=-1)
    return rms_norm(cq, q_lnorm), rms_norm(ckv, kv_lnorm), kr

def rope_tail(x, ang):
    return jnp.concatenate([x[..., :C_NOPE], apply_rope(x[..., C_NOPE:], ang)], axis=-1)

def mla_queries(cq, w_uq, q_norm, ang):
    b, n, _ = cq.shape
    q = rms_norm((cq @ w_uq).reshape(b, n, C_HEADS, C_QK), q_norm)
    if ang is not None:
        q = rope_tail(q, ang)
    return q[:, :, :, None, :]

def mla_keys_values(ckv, kr, w_ukv, k_norm, ang):
    b, n, _ = ckv.shape
    k_nope, v = jnp.split((ckv @ w_ukv).reshape(b, n, C_HEADS, C_NOPE + C_V), [C_NOPE], axis=-1)
    k = jnp.concatenate([k_nope, jnp.broadcast_to(kr[:, :, None, :], (b, n, C_HEADS, C_ROPE))], axis=-1)
    k = rms_norm(k, k_norm)
    if ang is not None:
        k = rope_tail(k, ang)
    return k, v

def setup_inputs(seed: int = 0) -> dict:
    key = jax.random.key(seed)
    ks = iter(jax.random.split(key, 64))

    def nrm(shape, s=1.0):
        return s * jax.random.normal(next(ks), shape, jnp.float32)

    def lin(shape):
        return nrm(shape, shape[-2] ** -0.5)

    def gain(shape):
        return 1.0 + nrm(shape, 0.05)

    D = D_MODEL
    qkv_a = (A_HEADS + 2 * A_KV_HEADS) * HEAD_DIM
    qkv_b = (B_HEADS + 2 * B_KV_HEADS) * HEAD_DIM
    qkv_d = 3 * D_HEADS * HEAD_DIM
    return {
        'x_prompt': nrm((BATCH, SEQ, D)),
        'x_sample': nrm((DEC_BATCH, DEC_SEQ, D)),
        'cache_a_k': nrm((DEC_BATCH, N_A, PAST_LEN, A_KV_HEADS, HEAD_DIM)),
        'cache_a_v': nrm((DEC_BATCH, N_A, PAST_LEN, A_KV_HEADS, HEAD_DIM)),
        'cache_b_k': nrm((DEC_BATCH, N_B, PAST_LEN, B_KV_HEADS, HEAD_DIM)),
        'cache_b_v': nrm((DEC_BATCH, N_B, PAST_LEN, B_KV_HEADS, HEAD_DIM)),
        'cache_c_kv': nrm((DEC_BATCH, N_C, PAST_LEN, C_KV_RANK)),
        'cache_c_krope': nrm((DEC_BATCH, N_C, PAST_LEN, C_ROPE)),
        'cache_d_k': nrm((DEC_BATCH, N_D, PAST_LEN, D_HEADS, HEAD_DIM)),
        'cache_d_v': nrm((DEC_BATCH, N_D, PAST_LEN, D_HEADS, HEAD_DIM)),
        'c': nrm((DEC_BATCH, D)),
        'c_ctx': nrm((D,)),
        'mod_w': nrm((DEPTH, D, N_MOD * D), 0.5 * D ** -0.5),
        'mod_b': nrm((DEPTH, N_MOD * D), 0.02),
        'norm_ff1': gain((DEPTH, D)),
        'norm_mix': gain((DEPTH, D)),
        'norm_ff2': gain((DEPTH, D)),
        'ff1_w_gu': lin((DEPTH, D, 2 * D_FF)),
        'ff1_w_down': lin((DEPTH, D_FF, D)),
        'ff2_w_gu': lin((DEPTH, D, 2 * D_FF)),
        'ff2_w_down': lin((DEPTH, D_FF, D)),
        'a_w_qkv': lin((N_A, D, qkv_a)),
        'a_q_norm': gain((N_A, HEAD_DIM)),
        'a_k_norm': gain((N_A, HEAD_DIM)),
        'a_sink': nrm((N_A, A_HEADS)),
        'a_w_o': lin((N_A, A_HEADS * HEAD_DIM, D)),
        'b_w_qkv': lin((N_B, D, qkv_b)),
        'b_q_norm': gain((N_B, HEAD_DIM)),
        'b_k_norm': gain((N_B, HEAD_DIM)),
        'b_w_o': lin((N_B, B_HEADS * HEAD_DIM, D)),
        'c_w_down': lin((N_C, D, C_Q_RANK + C_KV_RANK + C_ROPE)),
        'c_q_lnorm': gain((N_C, C_Q_RANK)),
        'c_kv_lnorm': gain((N_C, C_KV_RANK)),
        'c_w_uq': lin((N_C, C_Q_RANK, C_HEADS * C_QK)),
        'c_w_ukv': lin((N_C, C_KV_RANK, C_HEADS * (C_NOPE + C_V))),
        'c_q_norm': gain((N_C, C_QK)),
        'c_k_norm': gain((N_C, C_QK)),
        'c_w_o': lin((N_C, C_HEADS * C_V, D)),
        'd_w_qkv': lin((N_D, D, qkv_d)),
        'd_q_norm': gain((N_D, HEAD_DIM)),
        'd_k_norm': gain((N_D, HEAD_DIM)),
        'd_rpb': nrm((N_D, D_HEADS, 2 * NA_ROWS - 1, 2 * NA_COLS - 1), 0.5),
        'd_w_o': lin((N_D, D_HEADS * HEAD_DIM, D)),
    }

def reference(x_prompt, x_sample, cache_a_k, cache_a_v, cache_b_k, cache_b_v, cache_c_kv, cache_c_krope,
              cache_d_k, cache_d_v, c, c_ctx, mod_w, mod_b, norm_ff1, norm_mix, norm_ff2,
              ff1_w_gu, ff1_w_down, ff2_w_gu, ff2_w_down,
              a_w_qkv, a_q_norm, a_k_norm, a_sink, a_w_o,
              b_w_qkv, b_q_norm, b_k_norm, b_w_o,
              c_w_down, c_q_lnorm, c_kv_lnorm, c_w_uq, c_w_ukv, c_q_norm, c_k_norm, c_w_o,
              d_w_qkv, d_q_norm, d_k_norm, d_rpb, d_w_o):
    xp, xs = x_prompt, x_sample
    n_lat = xs.shape[1]
    ang_hd = grid_angles(n_lat, HEAD_DIM)
    ang_c = grid_angles(n_lat, C_ROPE)
    new_a_k, new_a_v, new_b_k, new_b_v = [], [], [], []
    new_c_kv, new_c_krope, new_d_k, new_d_v = [], [], [], []
    for i in range(DEPTH):
        kind, j = i % N_MIXERS, i // N_MIXERS
        mp = modulation(c_ctx, mod_w[i], mod_b[i])
        ms = [m[:, None, :] for m in modulation(c, mod_w[i], mod_b[i])]
        xp = half_ffn(xp, mp[0], mp[1], mp[2], norm_ff1[i], ff1_w_gu[i], ff1_w_down[i])
        xs = half_ffn(xs, ms[0], ms[1], ms[2], norm_ff1[i], ff1_w_gu[i], ff1_w_down[i])
        hp = modulate(xp, norm_mix[i], mp[3], mp[4])
        hs = modulate(xs, norm_mix[i], ms[3], ms[4])
        if kind == 0:
            q, k, v = gqa_project(hp, a_w_qkv[j], a_q_norm[j], a_k_norm[j], A_HEADS, A_KV_HEADS)
            op = merge_heads(block_attention(group_q(q, A_KV_HEADS), k, v, a_sink[j]), a_w_o[j])
            new_a_k.append(k)
            new_a_v.append(v)
            q, k, v = gqa_project(hs, a_w_qkv[j], a_q_norm[j], a_k_norm[j], A_HEADS, A_KV_HEADS)
            q, k = apply_rope(q, ang_hd), apply_rope(k, ang_hd)
            o = window_attention(group_q(q, A_KV_HEADS), k, v, cache_a_k[:, j], cache_a_v[:, j], a_sink[j])
            os_ = merge_heads(o, a_w_o[j])
        elif kind == 1:
            q, k, v = gqa_project(hp, b_w_qkv[j], b_q_norm[j], b_k_norm[j], B_HEADS, B_KV_HEADS)
            op = merge_heads(block_attention(group_q(q, B_KV_HEADS), k, v), b_w_o[j])
            new_b_k.append(k)
            new_b_v.append(v)
            q, k, v = gqa_project(hs, b_w_qkv[j], b_q_norm[j], b_k_norm[j], B_HEADS, B_KV_HEADS)
            q, k = apply_rope(q, ang_hd), apply_rope(k, ang_hd)
            k_all = jnp.concatenate([k, cache_b_k[:, j]], axis=1)
            v_all = jnp.concatenate([v, cache_b_v[:, j]], axis=1)
            os_ = merge_heads(block_attention(group_q(q, B_KV_HEADS), k_all, v_all), b_w_o[j])
        elif kind == 2:
            cq, ckv, kr = mla_compress(hp, c_w_down[j], c_q_lnorm[j], c_kv_lnorm[j])
            q = mla_queries(cq, c_w_uq[j], c_q_norm[j], None)
            k, v = mla_keys_values(ckv, kr, c_w_ukv[j], c_k_norm[j], None)
            op = merge_heads(block_attention(q, k, v), c_w_o[j])
            new_c_kv.append(ckv)
            new_c_krope.append(kr)
            cq, ckv, kr = mla_compress(hs, c_w_down[j], c_q_lnorm[j], c_kv_lnorm[j])
            q = mla_queries(cq, c_w_uq[j], c_q_norm[j], ang_c)
            k_l, v_l = mla_keys_values(ckv, kr, c_w_ukv[j], c_k_norm[j], ang_c)
            k_c, v_c = mla_keys_values(cache_c_kv[:, j], cache_c_krope[:, j], c_w_ukv[j], c_k_norm[j], None)
            o = block_attention(q, jnp.concatenate([k_l, k_c], axis=1), jnp.concatenate([v_l, v_c], axis=1))
            os_ = merge_heads(o, c_w_o[j])
        else:
            q, k, v = gqa_project(hp, d_w_qkv[j], d_q_norm[j], d_k_norm[j], D_HEADS, D_HEADS)
            op = merge_heads(block_attention(group_q(q, D_HEADS), k, v), d_w_o[j])
            new_d_k.append(k)
            new_d_v.append(v)
            q, k, v = gqa_project(hs, d_w_qkv[j], d_q_norm[j], d_k_norm[j], D_HEADS, D_HEADS)
            o = neighbourhood_attention(q, k, v, cache_d_k[:, j], cache_d_v[:, j], d_rpb[j])
            os_ = merge_heads(o, d_w_o[j])
        xp = xp + mp[5] * op
        xs = xs + ms[5] * os_
        xp = half_ffn(xp, mp[6], mp[7], mp[8], norm_ff2[i], ff2_w_gu[i], ff2_w_down[i])
        xs = half_ffn(xs, ms[6], ms[7], ms[8], norm_ff2[i], ff2_w_gu[i], ff2_w_down[i])
    y_prompt, y_sample = xp, xs
    s_a_k = jnp.stack(new_a_k, axis=1)
    s_a_v = jnp.stack(new_a_v, axis=1)
    s_b_k = jnp.stack(new_b_k, axis=1)
    s_b_v = jnp.stack(new_b_v, axis=1)
    s_c_kv = jnp.stack(new_c_kv, axis=1)
    s_c_krope = jnp.stack(new_c_krope, axis=1)
    s_d_k = jnp.stack(new_d_k, axis=1)
    s_d_v = jnp.stack(new_d_v, axis=1)
    return (y_prompt, y_sample, s_a_k, s_a_v, s_b_k, s_b_v, s_c_kv, s_c_krope, s_d_k, s_d_v)


_drawn_inputs = setup_inputs


def setup_inputs(seed=0):
    import zlib

    import numpy as np

    out = dict(_drawn_inputs(seed))
    spreads = {}
    factors = {'cache_a_k': 3.819,
     'cache_a_v': 2.941,
     'cache_b_k': 4.573,
     'cache_b_v': 3.545,
     'cache_c_kv': 3.988,
     'cache_c_krope': 7.441,
     'norm_ff1': 3.62,
     'norm_ff2': 3.917,
     'a_q_norm': 8.0,
     'a_sink': 8.0,
     'b_q_norm': 8.0,
     'c_q_lnorm': 8.0,
     'c_q_norm': 8.0,
     'c_k_norm': 8.0,
     'd_q_norm': 8.0,
     'd_rpb': 5.108}
    for name, (base, spread) in spreads.items():
        noise = np.random.default_rng([zlib.crc32(name.encode()), seed]).standard_normal(out[name].shape)
        drawn = base * np.exp(spread * noise) if base else spread * noise
        out[name] = __import__('jax').numpy.asarray(drawn.astype(out[name].dtype))
    for name, factor in factors.items():
        out[name] = (out[name] * factor).astype(out[name].dtype)
    return out
```

```python
from contextlib import ExitStack

import numpy as np

import concourse.bass as bass
from concourse import mybir

ALU = mybir.AluOpType
ACT = mybir.ActivationFunctionType
AX = mybir.AxisListType
F32 = mybir.dt.float32
F32R = mybir.dt.float32r

P = 128
D = 1024
KD = D // P
N_CTX = 128
N_LAT = 256
N_TOK = N_CTX + N_LAT
TT = N_TOK // P
N_PAST = 128
D_FF = 2816
KF = D_FF // P
DEPTH = 4
N_STAGE = 3 * DEPTH
HD = 64
HEADS = 16
KV_HEADS = 4
GRID_W = 64
GRID_H = N_LAT // GRID_W
A_WINDOW = 128
C_Q_RANK, C_KV_RANK, C_ROPE, C_NOPE = 384, 256, 32, 64
KQ, KC = C_Q_RANK // P, C_KV_RANK // P
C_QK = C_NOPE + C_ROPE
C_DOWN = C_Q_RANK + C_KV_RANK + C_ROPE
NA_ROWS, NA_COLS = 8, 16
RPB_R, RPB_C = 2 * NA_ROWS - 1, 2 * NA_COLS - 1
RPB_PAD = GRID_W - NA_COLS
RPB_W = RPB_C + 2 * RPB_PAD
RMS_EPS = 1e-6
ROPE_THETA = 10000.0
NEG = -1e30
FFN_RES = 0.5

GU_STEPS = KF
GU_CHUNK = KD * 2 * P
DN_STEPS = KD
DN_CHUNK = KF * P
WO_STEPS = KD // 2
WO_CHUNK = KD * 2 * P
QKV_W = 384
QKV_CHUNK = KD * QKV_W
QKT_BANKS = (6, 7, 5, 3)
C_BANKS = ((0, 1, 2), (3, 6, 7))
CT_BANKS = (0, 1, 2, 3, 5)
C_DOWN_COLS = (C_Q_RANK, C_KV_RANK + C_ROPE)
C_UQ_W, C_UKV_W = 2 * C_QK, 2 * 2 * HD
C_UP_CHUNK = KQ * C_UQ_W + KC * C_UKV_W
SLOT = QKV_CHUNK

N_PART = 9
SLABS = ((0, 1), (2, 3, 4), (5, 6, 7), ())
SLAB_SLOTS = 4
BOOT_BATCH, BOOT_SLOTS = 4, 4


B_NORM = 3
B_PART = 4
B_S = (0, 1, 2)
B_O = (3, 5)
B_PT = (6, 7)
GROUPS = {"A": 4, "B": 4, "C": 8, "D": 8}
HPG = {"A": 4, "B": 4, "C": 2, "D": 2}
KVPG = {"A": 1, "B": 1, "C": 2, "D": 2}


def stage_kind(s):
    return "ABCD"[(s // 3) % 4] if s % 3 == 1 else "F"


def chunk_base():
    per = {"F": GU_STEPS + DN_STEPS, "A": 4 + WO_STEPS, "B": 4 + WO_STEPS,
           "C": 2 + 8 + WO_STEPS, "D": 8 + WO_STEPS}
    base = [0]
    for s in range(N_STAGE):
        assert base[-1] % 2 == 0
        base.append(base[-1] + per[stage_kind(s)])
    return base


CB = chunk_base()


def first_part(s):
    return N_PART * (s // 3) + (3 if s % 3 == 0 else 8)


def n_parts(s):
    return 5 if s % 3 == 0 else 4 if s + 1 < N_STAGE else 1



def units(kind):
    return [("ctx", None, 0)] + [("lat", h, t) for h in range(HPG[kind]) for t in (1, 2)]


class Count:

    def __init__(self, sem, start=0):
        self.sem, self.n, self.at = sem, start, {}

    def mark(self, key, times=1):
        self.at[key] = self.n
        self.n += times

    def after(self, key, i=0):
        return self.at[key] + i + 1


class Chain:

    def __init__(self, eng, s):
        self.eng, self.sem, self.base, self.per, self.i, self.local = eng, s, 0, 0, None, 0

    def value(self):
        v = self.base + self.local
        return v if self.i is None else v + self.i * self.per

    def link(self, ins):
        ins.then_inc(self.sem, 1)
        self.local += 1
        self.eng.wait_ge(self.sem, self.value())

    def enter(self, i, per):
        self.base, self.local, self.i, self.per = self.base + self.local, 0, i, per

    def leave(self, rounds):
        assert self.local == self.per, (self.local, self.per)
        self.base, self.local, self.i, self.per = self.base + rounds * self.per, 0, None, 0


def qkt_types(kind):
    if kind in "AB":
        return [("q", 0, P), ("q", 1, P), ("k", 0, P)]
    if kind == "D":
        return [("q", 0, P), ("k", 0, P)]
    return [("q", 0, C_QK), ("q", 1, C_QK), ("k", 0, C_QK), ("k", 1, C_QK)]


def build(nc, a, out):
    with ExitStack() as ctx:
        def sb(name, shape, dt=F32):
            return ctx.enter_context(nc.sbuf_tensor(name, shape, dt))[:]

        def sem(name):
            return ctx.enter_context(nc.semaphore(name))

        ps = ctx.enter_context(nc.psum_tensor("ps", [P, 8, 512], F32))[:]

        x = sb("x", [P, KD, N_TOK])
        h_hi = sb("h_hi", [P, KD, N_TOK], F32R)
        h_lo = sb("h_lo", [P, KD, N_TOK], F32R)
        w_raw = [sb(f"w_raw{i}", [P, SLOT]) for i in range(2)]
        w_hi, scaled = [], []
        for i in range(2):
            with ExitStack() as tail:
                tail.enter_context(nc.sbuf_tensor(f"w_hi{i}_chunk", [P, GU_CHUNK], F32R))
                scaled.append(tail.enter_context(nc.sbuf_tensor(f"scaled{i}", [P, D], F32))[:])
            w_hi.append(sb(f"w_hi{i}", [P, SLOT], F32R))
        w_lo = [sb(f"w_lo{i}", [P, SLOT], F32R) for i in range(2)]
        slab = [sb(f"slab{i}", [P, D]) for i in range(2)] + [w[:, GU_CHUNK:GU_CHUNK + D] for w in w_raw]
        ident = sb("ident", [P, P])
        ones = sb("ones", [P, P])
        neghalf = sb("neghalf", [P, 16])
        cond = sb("cond", [P, KD, 2])
        mod_b = sb("mod_b", [P, DEPTH * N_PART * KD])
        gains = sb("gains", [P, N_STAGE, KD])
        mod = sb("mod", [P, N_PART * KD, 2])
        ssq = sb("ssq", [P, N_TOK])
        sq = [sb(f"sq{i}", [P, N_TOK]) for i in range(2)]
        rstd = sb("rstd", [P, 4])
        msq = sb("msq", [P, 4])
        diag = sb("diag", [P, TT, P])
        tmp = [sb(f"tmp{i}", [P, N_TOK]) for i in range(2)]

        cond_in = sem("cond_in")
        x_in = sem("x_in")
        consts_in = sem("consts_in")
        w_landed = [sem("w_landed0"), sem("w_landed1")]
        slab_landed = [sem(f"slab_landed{i}") for i in range(SLAB_SLOTS)]
        boot_landed = [sem(f"boot_landed{i}") for i in range(BOOT_SLOTS)]
        mixer_in = sem("mixer_in")
        w_split_hi = Count(sem("w_split_hi"))
        w_split_lo = Count(sem("w_split_lo"), 2)
        w_used = Count(sem("w_used"), 2)
        slab_scaled = sem("slab_scaled")
        slab_added = sem("slab_added")
        slab_summed = sem("slab_summed")
        part_turned = sem("part_turned")
        part_read = sem("part_read")
        act_ready = Count(sem("act_ready"), 2)
        x_updated = Count(sem("x_updated"), 2)
        sq_ready = Count(sem("sq_ready"))
        ssq_ready = Count(sem("ssq_ready"), 1)
        silu_ready = Count(sem("silu_ready"))
        act_hi_ready = Count(sem("act_hi_ready"))
        prod_ready = Count(sem("prod_ready"), 2)
        stats_made = Count(sem("stats_made"))
        ms_ready = Count(sem("ms_ready"))
        rstd_ready = Count(sem("rstd_ready"))
        diag_ready = Count(sem("diag_ready"))
        rbc_made = Count(sem("rbc_made"))
        xr_ready = Count(sem("xr_ready"))
        h_hi_ready = Count(sem("h_hi_ready"))
        h_ready = Count(sem("h_ready"))
        raw_ready = Count(sem("raw_ready"))
        rsq_ready = Count(sem("rsq_ready"))
        hms_ready = Count(sem("hms_ready"))
        hrs_ready = Count(sem("hrs_ready"))
        qn_ready = Count(sem("qn_ready"))
        qkt_made = Count(sem("qkt_made"))
        qkt_ready = Count(sem("qkt_ready"))
        s_made = Count(sem("s_made"))
        max_ready = Count(sem("max_ready"))
        exp_ready = Count(sem("exp_ready"))
        pt_made = Count(sem("pt_made"))
        pt_ready = Count(sem("pt_ready"))
        o_made = Count(sem("o_made"))
        o_ready = Count(sem("o_ready"))
        ot_made = Count(sem("ot_made"))
        ot_hi_ready = Count(sem("ot_hi_ready"))
        ot_ready = Count(sem("ot_ready"))
        wo_half = Count(sem("wo_half"))
        c_raw_ready = sem("c_raw_ready")
        c_rstd_ready = Count(sem("c_rstd_ready"))
        kr_ready = Count(sem("kr_ready"))
        c_norm_ready = Count(sem("c_norm_ready"))
        c_t_made = sem("c_t_made")
        c_hi_ready = sem("c_hi_ready")
        c_t_ready = sem("c_t_ready")
        bias_in = [sem("bias_in0"), sem("bias_in1")]
        out_done = sem("out_done")
        kv_out = sem("kv_out")
        pe_step, act_step, dve_step, pool_step = (sem(n) for n in ("pe_step", "act_step", "dve_step", "pool_step"))

        first_unit, kv_sent, n_kv = {}, {}, 0
        sq_ready.mark(-1, KD)
        ssq_ready.mark(-1, KD)
        for s in range(N_STAGE):
            kind = stage_kind(s)
            n_chunks = CB[s + 1] - CB[s]
            w_split_hi.mark(s, n_chunks)
            w_split_lo.mark(s, n_chunks)
            w_used.mark(s, n_chunks)
            if kind == "F":
                for c in (act_ready, silu_ready, act_hi_ready, prod_ready):
                    c.mark(s, GU_STEPS)
            else:
                first_unit[s] = s_made.n
                if kind == "C":
                    for key in ("ms", "kr", "cq"):
                        c_norm_ready.mark(key)
                    c_rstd_ready.mark("ms")
                for g in range(GROUPS[kind]):
                    if kind == "C":
                        kr_ready.mark((s, g))
                    raw_ready.mark((s, g))
                    rsq_ready.mark((s, g))
                    hms_ready.mark((s, g))
                    hrs_ready.mark((s, g))
                    qn_ready.mark((s, g))
                    types = len(qkt_types(kind))
                    qkt_made.mark((s, g), types)
                    qkt_ready.mark((s, g), types)
                    for u in range(len(units(kind))):
                        for c in (s_made, max_ready, exp_ready, pt_made, pt_ready, o_made, o_ready):
                            c.mark((s, g, u))
                    ot_made.mark((s, g))
                    ot_hi_ready.mark((s, g))
                    ot_ready.mark((s, g))
                wo_half.mark(s, WO_STEPS)
                for g in range(GROUPS[kind]):
                    n_kv += 32 if kind != "C" or g == 0 else 0
                    kv_sent[s, g] = n_kv
            kv_sent[s] = n_kv
            for c in (x_updated, sq_ready, ssq_ready):
                c.mark(s, KD)
            for c in (ms_ready, rstd_ready, diag_ready, rbc_made, stats_made):
                c.mark(s)
            for c in (xr_ready, h_hi_ready, h_ready):
                c.mark(s, KD)

        tiles = {}
        for kind in "FABCD":
            with ExitStack() as own:
                def part(name, shape, dt=F32):
                    return own.enter_context(nc.sbuf_tensor(f"{kind}_{name}", shape, dt))[:]

                v = tiles[kind] = {}
                if kind == "F":
                    v["acc"] = part("acc", [P, 2, D])
                    with ExitStack() as at_first:
                        v["boot"] = [at_first.enter_context(nc.sbuf_tensor(f"boot{i}", [P, BOOT_BATCH, D], F32))[:]
                                     for i in range(BOOT_SLOTS)]
                    v["act_hi"] = part("act_hi", [P, KF * N_TOK], F32R)
                    v["act_lo"] = part("act_lo", [P, KF * N_TOK], F32R)
                    continue
                w = C_UQ_W + C_UKV_W if kind == "C" else QKV_W
                nh = HPG[kind] + KVPG[kind]
                v["p"] = [part(f"p{i}", [P, 512]) for i in range(3)]
                v["pt"] = [part(f"pt{i}", [P, 512]) for i in range(2)]
                v["o"] = part("o", [P, TT, HPG[kind] * HD])
                v["stat"] = part("stat", [P, 3, 5, 4])
                v["rinv"] = part("rinv", [P, 4, 4])
                v["hms"] = part("hms", [P, 16])
                v["hrs"] = part("hrs", [P, 16])
                if kind == "C":
                    v["cat"] = part("cat", [P, 4, 4, C_QK])
                    v["sqc"] = part("sqc", [P, 4, 4, C_QK])
                    v["v"] = [part(f"v{i}", [P, 4, 2 * HD]) for i in range(2)]
                    v["cdn"] = part("cdn", [P, TT, C_DOWN])
                    v["kr"] = part("kr", [P, 4, C_ROPE])
                    v["junk"] = part("junk", [P, C_Q_RANK])
                    v["cms"] = part("cms", [P, 2, TT])
                    v["crs"] = part("crs", [P, 2, TT])
                    v["cqT_hi"] = part("cqT_hi", [P, KQ, N_TOK], F32R)
                    v["cqT_lo"] = part("cqT_lo", [P, KQ, N_TOK], F32R)
                    v["ckT_hi"] = part("ckT_hi", [P, KC, N_TOK + N_PAST], F32R)
                    v["ckT_lo"] = part("ckT_lo", [P, KC, N_TOK + N_PAST], F32R)
                    v["cache"] = part("cache", [P, KC, N_PAST])
                    v["gd"] = part("gd", [P, C_Q_RANK + C_KV_RANK])
                    v["g"] = part("g", [P, 2, C_QK])
                    v["cos"] = part("cos", [P, 2, C_ROPE])
                    v["sin"] = part("sin", [P, 2, C_ROPE])
                    v["rope"] = part("rope", [P, 2, 4, C_ROPE])
                    v["qt"] = part("qt", [P, 2, N_TOK])
                    v["kt"] = part("kt", [P, 2, N_TOK + N_PAST])
                    v["oT_hi"], v["oT_lo"] = h_hi, h_lo
                else:
                    v["raw"] = [part(f"raw{i}", [P, TT, QKV_W]) for i in range(2)]
                    v["nrm"] = part("nrm", [P, TT, nh * HD])
                    v["qn"] = part("qn", [P, TT, (HPG[kind] + 2) * HD])
                    v["g"] = part("g", [P, nh * HD])
                    v["qt"] = part("qt", [P, HPG[kind] // 2, N_TOK])
                    v["kt"] = part("kt", [P, 1, N_TOK])
                    v["ck"] = part("ck", [P, KV_HEADS if kind in "AB" else HEADS // 2, N_PAST])
                    v["cv"] = part("cv", [P, (KV_HEADS if kind in "AB" else HEADS) * HD])
                    v["oT_hi"] = part("oT_hi", [P, KD, N_TOK], F32R)
                    v["oT_lo"] = part("oT_lo", [P, KD, N_TOK], F32R)
                    if kind in "AB":
                        v["rope"] = part("rope", [P, 2, nh * HD])
                        v["cos"] = part("cos", [P, 2, HD])
                        v["sin"] = part("sin", [P, 2, HD])
                        v["cg"] = part("cg", [P, 2, nh * HD])
                        v["sg"] = part("sg", [P, 2, nh * HD])
                    if kind == "A":
                        v["mask"] = part("mask", [P, 2, P])
                        v["sink"] = part("sink", [P, HEADS])
                        v["sink8"] = part("sink8", [P, HEADS])
                    if kind == "D":
                        v["bias"] = [part(f"bias{i}", [P, 2, 6, GRID_W]) for i in range(2)]
                        v["mask"] = part("mask", [P, GRID_W])
        act_hi, act_lo = tiles["F"]["act_hi"], tiles["F"]["act_lo"]
        sil, prod = sq, tmp
        acc, boot = tiles["F"]["acc"], tiles["F"]["boot"]
        acc_of_scale = w_raw[1][:, 0:2 * D].rearrange("p (c d) -> p c d", c=2)

        mixer_loads = {
            "A": ["g", "cos", "sin", "mask", "sink", "ck", "cv"],
            "B": ["g", "cos", "sin", "ck", "cv"],
            "C": ["g", "gd", "cos", "sin", "cache", "kr"],
            "D": ["g", "mask", "ck", "cv"],
        }
        n_loads, total = {}, 0
        for kind in "ABCD":
            total += 16 * len(mixer_loads[kind])
            n_loads[kind] = total

        w_dram = {"gu": a["ffn_gu"], "dn": a["ffn_dn"]}
        scale_of = {"A": HD ** -0.5, "B": HD ** -0.5, "C": C_QK ** -0.5, "D": HD ** -0.5}
        n_down = {"A": 0, "B": 0, "C": 2, "D": 0}

        def chunk_src(s, c):
            kind, c = stage_kind(s), c - n_down[stage_kind(s)]
            if c < 0:
                return a["c_dn0" if c == -2 else "c_dn1"], KD * C_DOWN_COLS[c + 2]
            if c < GROUPS[kind]:
                return a[kind.lower() + "_w"][c], C_UP_CHUNK if kind == "C" else QKV_CHUNK
            return a[kind.lower() + "_wo"][c - GROUPS[kind]], WO_CHUNK

        def width(s, c):
            if c == CB[s + 1] - CB[s]:
                return width(s + 1, 0) if s + 1 < N_STAGE else 0
            if stage_kind(s) == "F":
                return GU_CHUNK if c < GU_STEPS else DN_CHUNK
            return chunk_src(s, c)[1]

        def landed(n):
            return 8 * n + 16

        def scaled_to(part, k):
            return KD * (part - 1) + k + 1

        def added_to(part, k):
            return (KD - 1) * (part - 1) + k

        def summed_to(part, k):
            return KD * part + k + 1

        block = ctx.enter_context(nc.Block())

        @block.sync
        def _(sp):
            def load_w(n, par, dst_w, src):
                sp.wait_ge(w_split_lo.sem, n + par + 1)
                sp.dma_start(w_raw[par][:, 0:dst_w], src).then_inc(w_landed[par], 16)

            def load_gu(s, j, par):
                f = 2 * (s // 3) + (s % 3 == 2)
                load_w(CB[s] + j - par, par, GU_CHUNK,
                       w_dram["gu"][bass.ds(f * GU_STEPS + j, 1)].rearrange("o p c -> (o p) c"))

            def load_slab(part, k):
                sp.wait_ge(slab_summed, summed_to(part, k) - SLAB_SLOTS)
                sp.dma_start(slab[k % SLAB_SLOTS][:], a["mod_w"][bass.ds(KD * part + k, 1)].rearrange(
                    "o p c -> (o p) c")).then_inc(slab_landed[k % SLAB_SLOTS], 16)

            def load_part(s, i):
                for q in range(4):
                    load_gu(s, 4 * i + q + 2, q % 2)
                    for k in SLABS[q]:
                        load_slab(first_part(s) + i, k)

            sp.dma_start(cond[:], a["cond"]).then_inc(cond_in, 16)
            for i in range(3 * KD // BOOT_BATCH):
                if i >= BOOT_SLOTS:
                    sp.wait_ge(slab_summed, BOOT_BATCH * (i - BOOT_SLOTS + 1))
                sp.dma_start(boot[i % BOOT_SLOTS][:], a["mod_w"][i * BOOT_BATCH:(i + 1) * BOOT_BATCH].rearrange(
                    "t p c -> p t c")).then_inc(boot_landed[i % BOOT_SLOTS], 16)
                if i == 1:
                    sp.dma_start(x[:], a["x"]).then_inc(x_in, 16)
                    for dst, name in ((ident, "ident"), (mod_b, "mod_b"), (gains, "gains")):
                        sp.dma_start(dst[:], a[name]).then_inc(consts_in, 16)
            for s in range(N_STAGE):
                f = 2 * (s // 3) + (s % 3 == 2)
                if stage_kind(s) == "F":
                    for par in range(2):
                        if s == 0 and par == 1:
                            sp.wait_ge(part_turned, 2)
                        load_gu(s, par, par)
                    load_part(s, 0)
                    if n_parts(s) > 1:
                        with sp.Fori(1, n_parts(s)) as i:
                            load_part(s, i)
                    if 2 * n_parts(s) + 1 < GU_STEPS // 2:
                        with sp.Fori(2 * n_parts(s) + 1, GU_STEPS // 2) as pair:
                            i = 2 * pair
                            for par in range(2):
                                load_gu(s, i + par, par)
                    sp.wait_ge(slab_summed, summed_to(first_part(s) + n_parts(s) - 1, KD - 1))
                    with sp.Fori(0, DN_STEPS // 2) as pair:
                        i = 2 * pair
                        for par in range(2):
                            load_w(CB[s] + GU_STEPS + i, par, DN_CHUNK,
                                   w_dram["dn"][bass.ds(f * DN_STEPS + i + par, 1)].rearrange("o p c -> (o p) c"))
                else:
                    for c in range(CB[s + 1] - CB[s]):
                        src, n = chunk_src(s, c)
                        load_w(CB[s] + c - c % 2, c % 2, n, src)
            sp.wait_ge(x_updated.sem, x_updated.after(N_STAGE - 1, KD - 1))
            sp.dma_start(out["y"], x[:]).then_inc(out_done, 16)
            sp.wait_ge(out_done, 16)

        @block.gpsimd
        def _(pool):
            pool.memset(ones[:], 1.0).then_inc(pool_step, 1)
            pool.memset(neghalf[:], -0.5).then_inc(pool_step, 1)
            pool.wait_ge(pool_step, 2)

            def power(dst, src, ready, key, done):
                pool.wait_ge(ready.sem, ready.after(key))
                n = src.shape[1]
                pool.tensor_tensor(dst, src, neghalf[:, 0:n], ALU.pow).then_inc(done.sem, 1)

            def add_slab(part, k, sums):
                pool.wait_ge(slab_scaled, scaled_to(part, k))
                if k > 1:
                    pool.wait_ge(slab_added, added_to(part, k - 1))
                pool.tensor_tensor(sums[:, 0, :], sums[:, 0, :], scaled[k % 2][:], ALU.add).then_inc(slab_added, 1)

            for part, sums in ((1, acc_of_scale), (2, acc)):
                for k in range(1, KD):
                    add_slab(part, k, sums)
            for s in range(N_STAGE):
                kind = stage_kind(s)
                power(rstd[:, 0:TT], msq[:, 0:TT], ms_ready, s, rstd_ready)
                if kind == "F":
                    for k in range(1, KD):
                        add_slab(first_part(s), k, acc)
                    if n_parts(s) > 1:
                        with pool.Fori(1, n_parts(s)) as i:
                            for k in range(1, KD):
                                add_slab(first_part(s) + i, k, acc)
                    continue
                v = tiles[kind]
                pool.wait_ge(w_used.sem, w_used.at[s])
                for name in mixer_loads[kind]:
                    dst = v[name][:, 3, :] if name == "kr" else v[name][:]
                    pool.dma_start(dst, a[f"{kind.lower()}_{name}"]).then_inc(mixer_in, 16)

                def load_bias(g):
                    if g >= 2:
                        pool.wait_ge(qkt_made.sem, qkt_made.after((s, g - 1)))
                    for rl in range(2):
                        for h in range(2):
                            src = a["d_rpb"]
                            at = ((2 * g + h) * RPB_R + 5 - rl) * RPB_W
                            pool.dma_start(v["bias"][g % 2][GRID_W * rl:GRID_W * (rl + 1), h],
                                           bass.AP(tensor=src.tensor, offset=src.offset + at,
                                                   ap=[[1, GRID_W], [RPB_W, 6], [1, GRID_W]])
                                           ).then_inc(bias_in[g % 2], 16)

                if kind == "D":
                    load_bias(0)
                    load_bias(1)
                if kind == "C":
                    power(v["crs"].rearrange("p a b -> p (a b)"), v["cms"].rearrange("p a b -> p (a b)"),
                          c_norm_ready, "ms", c_rstd_ready)
                    pool.wait_ge(c_norm_ready.sem, c_norm_ready.after("cq"))
                    for name, src in (("new_c_kv", v["cdn"][:, 0, C_Q_RANK:C_Q_RANK + C_KV_RANK]),
                                      ("new_c_krope", v["cdn"][:, 0, C_Q_RANK + C_KV_RANK:C_DOWN])):
                        pool.dma_start(out[name], src).then_inc(kv_out, 16)
                for g in range(GROUPS[kind]):
                    nh = {"A": 15, "B": 15, "C": 14, "D": 12}[kind]
                    if kind == "C":
                        if g >= 1:
                            pool.wait_ge(qkt_made.sem, qkt_made.after((s, g - 1), 3))
                        else:
                            pool.wait_ge(c_norm_ready.sem, c_norm_ready.after("kr"))
                            pool.wait_ge(mixer_in, n_loads[kind])
                        for h in (2, 3):
                            ins = pool.tensor_copy(v["cat"][:, :, h, C_NOPE:C_QK], v["kr"][:])
                        ins.then_inc(kr_ready.sem, 1)
                    power(v["hrs"][:, 0:nh], v["hms"][:, 0:nh], hms_ready, (s, g), hrs_ready)
                    if kind == "D" and 1 <= g and g + 1 < GROUPS[kind]:
                        load_bias(g + 1)
                    if kind != "C":
                        kw = KVPG[kind] * HD
                        pool.wait_ge(qn_ready.sem, qn_ready.after((s, g)))
                        pool.dma_start(out[f"new_{kind.lower()}_k"][:, g * kw:(g + 1) * kw],
                                       v["qn"][:, 0, HPG[kind] * HD:HPG[kind] * HD + kw]).then_inc(kv_out, 16)
                        pool.dma_start(out[f"new_{kind.lower()}_v"][:, g * kw:(g + 1) * kw],
                                       v["raw"][g % 2][:, 0, QKV_W - kw:QKV_W]).then_inc(kv_out, 16)
            pool.wait_ge(kv_out, kv_sent[N_STAGE - 1])

        @block.tensor
        def _(pe):
            chain = Chain(pe, pe_step)
            pe.sem_inc(w_used.sem, 2)

            def turn_part(part, sums):
                pe.wait_ge(slab_summed, summed_to(part, KD - 1))
                if not isinstance(part, int) or part > 0:
                    pe.wait_ge(slab_added, added_to(part, KD - 1))
                    pe.wait_ge(part_read, part)
                for i in range(2 * KD):
                    mm = pe.transpose(ps[:, B_PART + i // 4, i % 4 * P:(i % 4 + 1) * P],
                                      sums.rearrange("p c d -> p (c d)")[:, i * P:(i + 1) * P], ident[:])
                mm.then_inc(part_turned, 1)

            def norm(s):
                pe.wait_ge(ssq_ready.sem, ssq_ready.after(s - 1, KD - 1))
                for t in range(TT):
                    mm = pe.matmul(ps[:, B_NORM, t:t + 1], ssq[:, t * P:(t + 1) * P], ones[:, 0:1],
                                   start=True, stop=True)
                mm.then_inc(stats_made.sem, 1)
                pe.wait_ge(diag_ready.sem, diag_ready.after(s))
                pe.matmul(ps[:, B_NORM, 0:N_TOK], ones[:], diag.rearrange("p t c -> p (t c)"),
                          start=True, stop=True).then_inc(rbc_made.sem, 1)

            def gu_first(s):
                pe.wait_ge(w_split_lo.sem, w_split_lo.after(s, 0))
                w = [q[0][:, 0:GU_CHUNK].rearrange("p (k u c) -> p k u c", k=KD, u=2) for q in (w_hi, w_lo)]
                for k in range(KD):
                    pe.wait_ge(h_ready.sem, h_ready.after(s, k))
                    for u in range(2):
                        for i, (lh, rh) in enumerate(((w[0], h_hi), (w[0], h_lo), (w[1], h_hi))):
                            mm = pe.matmul(ps[:, u, 0:N_TOK], lh[:, k, u, :], rh[:, k, :],
                                           start=(k == 0 and i == 0), stop=(k == KD - 1 and i == 2))
                mm.then_inc(w_used.sem, 1)

            def gu_step(s, j, par):
                pe.wait_ge(w_split_hi.sem, w_split_hi.after(s, j))
                pe.wait_ge(prod_ready.sem, prod_ready.at[s] + j - 1)
                w = [q[par][:, 0:GU_CHUNK].rearrange("p (k u c) -> p k u c", k=KD, u=2) for q in (w_hi, w_lo)]
                for u in range(2):
                    for k in range(KD):
                        for h in (h_hi, h_lo):
                            pe.matmul(ps[:, 2 * par + u, 0:N_TOK], w[0][:, k, u, :], h[:, k, :],
                                      start=(k == 0 and h is h_hi), stop=False)
                pe.wait_ge(w_split_lo.sem, w_split_lo.after(s, j))
                for u in range(2):
                    for k in range(KD):
                        mm = pe.matmul(ps[:, 2 * par + u, 0:N_TOK], w[1][:, k, u, :], h_hi[:, k, :],
                                       start=False, stop=(k == KD - 1))
                mm.then_inc(w_used.sem, 1)

            def dn_step(s, m, par, first=False):
                c = GU_STEPS + m
                pe.wait_ge(w_split_hi.sem, w_split_hi.after(s, c))
                pe.wait_ge(x_updated.sem, x_updated.at[s] + m - 1)
                if first:
                    pe.wait_ge(prod_ready.sem, prod_ready.after(s, GU_STEPS - 2))
                    pe.wait_ge(act_ready.sem, act_ready.after(s, KF - 3))
                for k in range(KF):
                    if first and k >= KF - 2:
                        pe.wait_ge(act_ready.sem, act_ready.after(s, k))
                    for y in (act_hi, act_lo):
                        pe.matmul(ps[:, par, 0:N_TOK], w_hi[par][:, k * P:(k + 1) * P],
                                  y[:, k * N_TOK:(k + 1) * N_TOK], start=(k == 0 and y is act_hi), stop=False)
                pe.wait_ge(w_split_lo.sem, w_split_lo.after(s, c))
                for k in range(KF):
                    mm = pe.matmul(ps[:, par, 0:N_TOK], w_lo[par][:, k * P:(k + 1) * P],
                                   act_hi[:, k * N_TOK:(k + 1) * N_TOK], start=False, stop=(k == KF - 1))
                mm.then_inc(w_used.sem, 1)

            def split_product(bank, cols, left, right, n, rows=P):
                for k in range(n):
                    for i, (lh, rh) in enumerate(((0, 0), (0, 1), (1, 0))):
                        mm = pe.matmul(ps[0:rows, bank, cols[0]:cols[1]], left(lh, k), right(rh, k),
                                       start=(k == 0 and i == 0), stop=(k == n - 1 and i == 2))
                return mm

            def projection(s, g):
                kind = stage_kind(s)
                v = tiles[kind]
                c = n_down[kind] + g
                par = c % 2
                pe.wait_ge(w_split_hi.sem, w_split_hi.after(s, c))
                pe.wait_ge(w_split_lo.sem, w_split_lo.after(s, c))
                if g >= 2:
                    pe.wait_ge(exp_ready.sem, exp_ready.after((s, g - 2, len(units(kind)) - 1)))
                    pe.wait_ge(ot_ready.sem, ot_ready.after((s, g - 2)))
                if g >= 1:
                    pe.wait_ge(raw_ready.sem, raw_ready.after((s, g - 1)))
                    pe.wait_ge(qkt_ready.sem, qkt_ready.after((s, g - 1), len(qkt_types(kind)) - 1))
                if kind != "C" and g == 0:
                    for k in range(KD):
                        pe.wait_ge(h_ready.sem, h_ready.after(s, k))
                        for t in range(TT):
                            for i, (lh, rh) in enumerate(((h_hi, w_hi), (h_hi, w_lo), (h_lo, w_hi))):
                                mm = pe.matmul(ps[:, t, 0:QKV_W], lh[:, k, t * P:(t + 1) * P],
                                               rh[par][:, k * QKV_W:(k + 1) * QKV_W],
                                               start=(k == 0 and i == 0), stop=(k == KD - 1 and i == 2))
                elif kind != "C":
                    for t in range(TT):
                        mm = split_product(
                            t, (0, QKV_W),
                            lambda i, k: (h_hi, h_lo)[i][:, k, t * P:(t + 1) * P],
                            lambda i, k: (w_hi, w_lo)[i][par][:, k * QKV_W:(k + 1) * QKV_W], KD)
                else:
                    for t in range(4):
                        if t < TT:
                            split_product(
                                t, (0, C_UQ_W),
                                lambda i, k: (v["cqT_hi"], v["cqT_lo"])[i][:, k, t * P:(t + 1) * P],
                                lambda i, k: (w_hi, w_lo)[i][par][:, k * C_UQ_W:(k + 1) * C_UQ_W], KQ)
                        at = KQ * C_UQ_W
                        mm = split_product(
                            t, (C_UQ_W, C_UQ_W + C_UKV_W),
                            lambda i, k: (v["ckT_hi"], v["ckT_lo"])[i][:, k, t * P:(t + 1) * P],
                            lambda i, k: (w_hi, w_lo)[i][par][:, at + k * C_UKV_W:at + (k + 1) * C_UKV_W], KC)
                mm.then_inc(w_used.sem, 1)

            def turn_qk(s, g):
                kind = stage_kind(s)
                v = tiles[kind]
                pe.wait_ge(qn_ready.sem, qn_ready.after((s, g)))
                if g >= 1:
                    n = len(units(kind))
                    pe.wait_ge(o_ready.sem, o_ready.after((s, g - 1, n - 1)))
                for i, (what, n, w) in enumerate(qkt_types(kind)):
                    bank = QKT_BANKS[i]
                    if kind == "C":
                        col = n + (2 if what == "k" else 0)
                        for t in range(4 if what == "k" else TT):
                            mm = pe.transpose(ps[0:w, bank, t * P:(t + 1) * P], v["cat"][:, t, col, :], ident[:])
                    else:
                        at = n * P if what == "q" else HPG[kind] * HD
                        for t in range(TT):
                            mm = pe.transpose(ps[:, bank, t * P:(t + 1) * P], v["qn"][:, t, at:at + P], ident[:])
                    mm.then_inc(qkt_made.sem, 1)

            def scores(s, g, u, uu):
                kind = stage_kind(s)
                v = tiles[kind]
                what, h, t = units(kind)[u]
                bank = B_S[uu % 3]
                if u == 0:
                    pe.wait_ge(qkt_ready.sem, qkt_ready.after((s, g), len(qkt_types(kind)) - 1))
                if uu >= 3:
                    pe.wait_ge(exp_ready.sem, exp_ready.at[(s, g, u)] - 2)
                if g + 1 < GROUPS[kind]:
                    pe.wait_ge(raw_ready.sem, raw_ready.after((s, g + 1)))
                heads = (h,)
                if what == "ctx":
                    heads = sorted(range(HPG[kind]), key=lambda h: h % 2)
                for h in heads:
                    if kind == "C":
                        q = v["qt"][0:C_QK, h, t * P:(t + 1) * P]
                        k = v["kt"][0:C_QK, h, :]
                    else:
                        half = slice(HD * (h % 2), HD * (h % 2) + HD)
                        q = v["qt"][half, h // 2, t * P:(t + 1) * P]
                        k = v["kt"][half, 0, :]
                    if what == "ctx":
                        mm = pe.matmul(ps[:, bank, h * P:(h + 1) * P], q, k[:, 0:P], start=True, stop=True)
                        if kind != "C" and h == HPG[kind] - 2:
                            chain.link(mm)
                    elif kind == "C":
                        mm = pe.matmul(ps[:, bank, 0:N_LAT + N_PAST], q, k[:, P:P + N_LAT + N_PAST],
                                       start=True, stop=True)
                    else:
                        cache = v["ck"][half, g, :]
                        pe.matmul(ps[:, bank, 0:N_LAT], q, k[:, P:P + N_LAT], start=True, stop=True)
                        mm = pe.matmul(ps[:, bank, N_LAT:N_LAT + N_PAST], q, cache, start=True, stop=True)
                mm.then_inc(s_made.sem, 1)

            def turn_p(s, g, u, uu):
                kind = stage_kind(s)
                what, _, _ = units(kind)[u]
                pe.wait_ge(exp_ready.sem, exp_ready.after((s, g, u)))
                if u >= 2:
                    pe.wait_ge(pt_ready.sem, pt_ready.at[(s, g, u)] - 1)
                for n in range(HPG[kind] if what == "ctx" else 3):
                    mm = pe.transpose(ps[:, B_PT[uu % 2], n * P:(n + 1) * P],
                                      tiles[kind]["p"][uu % 3][:, n * P:(n + 1) * P], ident[:])
                mm.then_inc(pt_made.sem, 1)

            def values(s, g, u, uu):
                kind = stage_kind(s)
                v = tiles[kind]
                what, h, t = units(kind)[u]
                pt, bank = v["pt"][uu % 2], B_O[uu % 2]
                pe.wait_ge(pt_ready.sem, pt_ready.after((s, g, u)))
                if u >= 2:
                    pe.wait_ge(o_ready.sem, o_ready.at[(s, g, u)] - 1)
                elif g >= 1:
                    pe.wait_ge(ot_ready.sem, ot_ready.after((s, g - 1)))

                def val(t, h):
                    if kind == "C":
                        return v["v"][g % 2][:, t, h * HD:(h + 1) * HD]
                    kvh = h * KVPG[kind] // HPG[kind]
                    at = QKV_W - KVPG[kind] * HD + kvh * HD
                    if t == 3:
                        at = (g * KVPG[kind] + kvh) * HD
                        return v["cv"][:, at:at + HD]
                    return v["raw"][g % 2][:, t, at:at + HD]

                if what == "ctx":
                    for h in range(HPG[kind]):
                        mm = pe.matmul(ps[:, bank, h * HD:(h + 1) * HD], pt[:, h * P:(h + 1) * P], val(0, h),
                                       start=True, stop=True)
                else:
                    for n in range(3):
                        mm = pe.matmul(ps[:, bank, 0:HD], pt[:, n * P:(n + 1) * P], val(n + 1, h),
                                       start=(n == 0), stop=(n == 2))
                mm.then_inc(o_made.sem, 1)

            def turn_o(s, g):
                kind = stage_kind(s)
                pe.wait_ge(o_ready.sem, o_ready.after((s, g, len(units(kind)) - 1)))
                if g + 1 < GROUPS[kind]:
                    pe.wait_ge(qkt_ready.sem, qkt_ready.after((s, g + 1), len(qkt_types(kind)) - 1))
                for n in range(HPG[kind] // 2):
                    for t in range(TT):
                        mm = pe.transpose(ps[:, B_O[n], t * P:(t + 1) * P],
                                          tiles[kind]["o"][:, t, n * P:(n + 1) * P], ident[:])
                mm.then_inc(ot_made.sem, 1)

            def compress(s):
                v = tiles["C"]
                for c in range(2):
                    w = C_DOWN_COLS[c]
                    pe.wait_ge(w_split_hi.sem, w_split_hi.after(s, c))
                    pe.wait_ge(w_split_lo.sem, w_split_lo.after(s, c))
                    if c == 0:
                        for k in range(KD):
                            pe.wait_ge(h_ready.sem, h_ready.after(s, k))
                            for t in range(TT):
                                for i, (lh, rh) in enumerate(((h_hi, w_hi), (h_hi, w_lo), (h_lo, w_hi))):
                                    mm = pe.matmul(ps[:, C_BANKS[0][t], 0:w], lh[:, k, t * P:(t + 1) * P],
                                                   rh[0][:, k * w:(k + 1) * w],
                                                   start=(k == 0 and i == 0), stop=(k == KD - 1 and i == 2))
                        mm.then_inc(w_used.sem, 1)
                        continue
                    for t in range(TT):
                        mm = split_product(
                            C_BANKS[c][t], (0, w),
                            lambda i, k: (h_hi, h_lo)[i][:, k, t * P:(t + 1) * P],
                            lambda i, k: (w_hi, w_lo)[i][c][:, k * w:(k + 1) * w], KD)
                    mm.then_inc(w_used.sem, 1)
                pe.wait_ge(c_norm_ready.sem, c_norm_ready.after("cq"))
                for n in range(KQ + KC):
                    for t in range(TT):
                        mm = pe.transpose(ps[:, CT_BANKS[n], t * P:(t + 1) * P],
                                          v["cdn"][:, t, n * P:(n + 1) * P], ident[:])
                    mm.then_inc(c_t_made, 1)
                pe.wait_ge(c_t_ready, KQ + KC + 1)

            pe.wait_ge(pool_step, 2)
            pe.wait_ge(consts_in, 16 * 3)
            for part in range(3):
                turn_part(part, acc_of_scale if part == 1 else acc)
            uu = 0
            for s in range(N_STAGE):
                norm(s)
                kind = stage_kind(s)
                if kind == "F":
                    gu_first(s)
                    for j in range(1, 4):
                        gu_step(s, j, j % 2)
                    turn_part(first_part(s), acc)
                    if n_parts(s) > 1:
                        with pe.Fori(1, n_parts(s)) as i:
                            for q in range(4):
                                gu_step(s, 4 * i + q, q % 2)
                            turn_part(first_part(s) + i, acc)
                    with pe.Fori(2 * n_parts(s), GU_STEPS // 2) as pair:
                        i = 2 * pair
                        for par in range(2):
                            gu_step(s, i + par, par)
                    dn_step(s, 0, 0, True)
                    dn_step(s, 1, 1)
                    with pe.Fori(1, DN_STEPS // 2) as pair:
                        i = 2 * pair
                        for par in range(2):
                            dn_step(s, i + par, par)
                    continue
                n_g, n_u = GROUPS[kind], len(units(kind))
                pe.wait_ge(mixer_in, n_loads[kind])
                if kind == "C":
                    compress(s)
                projection(s, 0)
                turn_qk(s, 0)
                for g in range(n_g):
                    if g + 1 < n_g:
                        projection(s, g + 1)
                    for u in range(n_u + 3):
                        if u < n_u:
                            scores(s, g, u, uu + u)
                        if 2 <= u < n_u + 2:
                            turn_p(s, g, u - 2, uu + u - 2)
                        if u >= 3:
                            values(s, g, u - 3, uu + u - 3)
                    uu += n_u
                    if g + 1 < n_g:
                        turn_qk(s, g + 1)
                    turn_o(s, g)
                pe.wait_ge(ot_ready.sem, ot_ready.after((s, n_g - 1)))
                v = tiles[kind]
                for c in range(WO_STEPS):
                    n = n_down[kind] + n_g + c
                    par = n % 2
                    pe.wait_ge(w_split_hi.sem, w_split_hi.after(s, n))
                    pe.wait_ge(w_split_lo.sem, w_split_lo.after(s, n))
                    for b in range(2):
                        pe.wait_ge(x_updated.sem, x_updated.at[s] + 2 * c + b - 1)
                        at = lambda k: slice(k * 2 * P + b * P, k * 2 * P + (b + 1) * P)
                        mm = split_product(b, (0, N_TOK),
                                           lambda i, k: (w_hi, w_lo)[i][par][:, at(k)],
                                           lambda i, k: (v["oT_hi"], v["oT_lo"])[i][:, k, :], KD)
                        mm.then_inc(wo_half.sem if b == 0 else w_used.sem, 1)

        @block.scalar
        def _(act):
            chain = Chain(act, act_step)

            def split_hi(n, par, w):
                act.wait_ge(w_landed[par], landed(n))
                act.wait_ge(w_used.sem, n + par + 1)
                act.activation(w_hi[par][:, 0:w], w_raw[par][:, 0:w], ACT.Copy).then_inc(w_split_hi.sem, 1)

            def modulated_hi(s, k):
                act.wait_ge(xr_ready.sem, xr_ready.after(s, k))
                shift = mod[:, 3 * KD * (s % 3) + k, :]
                act.activation(h_hi[:, k, 0:P], tmp[k % 2][:, 0:P], ACT.Identity, bias=shift[:, 0:1])
                act.activation(h_hi[:, k, P:N_TOK], tmp[k % 2][:, P:N_TOK], ACT.Identity,
                               bias=shift[:, 1:2]).then_inc(h_hi_ready.sem, 1)

            def scale_slab(part, k, w, sums):
                if k == 0:
                    act.wait_ge(part_turned, part)
                elif k > 2:
                    act.wait_ge(slab_added, added_to(part, k - 2))
                act.activation(sums[:, 0, :] if k == 0 else scaled[k % 2][:], w, ACT.Copy,
                               scale=cond[:, k, 0:1]).then_inc(slab_scaled, 1)

            def square(s, m, par):
                act.wait_ge(x_updated.sem, x_updated.after(s, m))
                act.activation(sq[par][:], x[:, m, :] if isinstance(m, int) else
                               x[:, bass.ds(m, 1), :].rearrange("p o t -> p (o t)"),
                               ACT.Square).then_inc(sq_ready.sem, 1)

            def gu_step(s, j, par, w_next, part=None, slabs=()):
                def scale_next(ks):
                    for k in ks:
                        act.wait_ge(slab_landed[k % SLAB_SLOTS], 32 * (part - 3) + 16 * (k // SLAB_SLOTS + 1))
                        scale_slab(part, k, slab[k % SLAB_SLOTS], acc)

                split_hi(CB[s] + j + 1 - (1 - par), 1 - par, w_next)
                scale_next(slabs[0:2])
                act.wait_ge(w_used.sem, w_used.after(s, j))
                act.activation(sil[par][:], ps[:, 2 * par, 0:N_TOK], ACT.Silu).then_inc(silu_ready.sem, 1)
                act.wait_ge(prod_ready.sem, prod_ready.after(s, j))
                act.activation(act_hi[:, bass.ds(j * N_TOK, N_TOK)], prod[par][:],
                               ACT.Copy).then_inc(act_hi_ready.sem, 1)
                scale_next(slabs[2:])

            def dn_step(s, m, par, w_next):
                if w_next:
                    split_hi(CB[s] + GU_STEPS + m + 1 - (1 - par), 1 - par, w_next)
                square(s, m, par)

            def raw(s, g):
                kind = stage_kind(s)
                v = tiles[kind]
                act.wait_ge(w_used.sem, w_used.after(s, n_down[kind] + g))
                if g >= 2 and kind != "C":
                    act.wait_ge(kv_out, kv_sent[s, g - 1])
                if kind != "C":
                    nn = (HPG[kind] + KVPG[kind]) * HD
                    act.activation(v["raw"][g % 2][:], ps[:, 0:TT, 0:QKV_W], ACT.Copy).then_inc(raw_ready.sem, 1)
                    act.wait_ge(raw_ready.sem, raw_ready.after((s, g)))
                    act.activation(v["nrm"][:], v["raw"][g % 2][:, :, 0:nn], ACT.Square).then_inc(rsq_ready.sem, 1)
                    return
                act.wait_ge(kr_ready.sem, kr_ready.after((s, g)))
                kv = ps[:, 0:4, C_UQ_W:C_UQ_W + C_UKV_W].rearrange("p t (h x d) -> p t h x d", h=2, x=2)
                act.activation(v["cat"][:, 0:TT, 0:2, :].rearrange("p t h d -> p t (h d)"),
                               ps[:, 0:TT, 0:C_UQ_W], ACT.Copy)
                act.activation(v["v"][g % 2].rearrange("p t (h d) -> p t h d", h=2), kv[:, :, :, 1, :], ACT.Copy)
                act.activation(v["cat"][:, :, 2:4, 0:C_NOPE], kv[:, :, :, 0, :], ACT.Copy).then_inc(raw_ready.sem, 1)
                act.wait_ge(raw_ready.sem, raw_ready.after((s, g)))
                act.activation(v["sqc"][:, 0:TT, 0:2, :], v["cat"][:, 0:TT, 0:2, :], ACT.Square)
                act.activation(v["sqc"][:, :, 2:4, :], v["cat"][:, :, 2:4, :], ACT.Square).then_inc(rsq_ready.sem, 1)

            def qk_copies(s, g):
                kind = stage_kind(s)
                v = tiles[kind]
                for i, (what, n, w) in enumerate(qkt_types(kind)):
                    act.wait_ge(qkt_made.sem, qkt_made.after((s, g), i))
                    dst = v["kt" if what == "k" else "qt"][0:w, n if what == "q" or kind == "C" else 0, :]
                    act.activation(dst, ps[0:w, QKT_BANKS[i], 0:dst.shape[1]], ACT.Copy).then_inc(qkt_ready.sem, 1)

            def probabilities(s, g, u, uu):
                kind = stage_kind(s)
                v = tiles[kind]
                what, h, t = units(kind)[u]
                st, p = v["stat"], v["p"][uu % 3]
                act.wait_ge(max_ready.sem, max_ready.after((s, g, u)))
                if uu >= 3 and uu - 3 >= first_unit[s]:
                    act.wait_ge(pt_made.sem, pt_made.at[(s, g, u)] - 2)
                n = HPG[kind] if what == "ctx" else 1
                w = P if what == "ctx" else N_LAT + N_PAST
                for i in range(n):
                    ins = act.activation(p[:, i * w:(i + 1) * w], ps[:, B_S[uu % 3], i * w:(i + 1) * w], ACT.Exp,
                                         bias=st[:, uu % 3, 1, i:i + 1], scale=scale_of[kind],
                                         accum_out=st[:, uu % 3, 2, i:i + 1])
                if kind == "A":
                    ins = act.activation(st[:, uu % 3, 3, 0:n], st[:, uu % 3, 3, 0:n], ACT.Exp)
                ins.then_inc(exp_ready.sem, 1)

            def p_copy(s, g, u, uu):
                kind = stage_kind(s)
                what, _, _ = units(kind)[u]
                w = P * (HPG[kind] if what == "ctx" else 3)
                act.wait_ge(pt_made.sem, pt_made.after((s, g, u)))
                if uu - 2 >= first_unit[s]:
                    act.wait_ge(o_made.sem, o_made.at[(s, g, u)] - 1)
                act.activation(tiles[kind]["pt"][uu % 2][:, 0:w], ps[:, B_PT[uu % 2], 0:w],
                               ACT.Copy).then_inc(pt_ready.sem, 1)

            def o_hi(s, g):
                kind = stage_kind(s)
                v = tiles[kind]
                act.wait_ge(ot_made.sem, ot_made.after((s, g)))
                for n in range(HPG[kind] // 2):
                    ins = act.activation(v["oT_hi"][:, g * HPG[kind] // 2 + n, :], ps[:, B_O[n], 0:N_TOK], ACT.Copy)
                ins.then_inc(ot_hi_ready.sem, 1)

            def compress(s):
                v = tiles["C"]
                for c in range(2):
                    split_hi(CB[s] + 2 * c, 1 - c, width(s, c + 1))
                    act.wait_ge(w_used.sem, w_used.after(s, c))
                    w, at = C_DOWN_COLS[c], C_Q_RANK * c
                    for t in range(TT):
                        chain.link(act.activation(v["cdn"][:, t, at:at + w], ps[:, C_BANKS[c][t], 0:w], ACT.Copy))
                    for t in range(TT):
                        w = (C_Q_RANK, C_KV_RANK)[c]
                        chain.link(act.activation(v["junk"][:, 0:w], v["cdn"][:, t, at:at + w], ACT.Square,
                                                  accum_out=v["cms"][:, c, t:t + 1]))
                act.sem_inc(c_raw_ready, 1)
                for n in range(KQ + KC):
                    act.wait_ge(c_t_made, n + 1)
                    dst = v["cqT_hi"][:, n, :] if n < KQ else v["ckT_hi"][:, n - KQ, 0:N_TOK]
                    act.activation(dst, ps[:, CT_BANKS[n], 0:N_TOK], ACT.Copy).then_inc(c_hi_ready, 1)
                act.wait_ge(mixer_in, n_loads["C"])
                act.activation(v["ckT_hi"][:, :, N_TOK:N_TOK + N_PAST], v["cache"][:], ACT.Copy).then_inc(c_hi_ready, 1)

            def squares():
                for m in range(KD):
                    if m >= 2:
                        act.wait_ge(ssq_ready.sem, ssq_ready.after(-1, m - 2))
                    act.activation(sq[m % 2][:], x[:, m, :], ACT.Square).then_inc(sq_ready.sem, 1)

            act.wait_ge(cond_in, 16)
            chain.link(act.activation(cond[:], cond[:], ACT.Silu))
            for part, sums in ((1, acc_of_scale), (2, acc)):
                for k in range(KD):
                    n = part * KD + k
                    batch = n // BOOT_BATCH
                    act.wait_ge(boot_landed[batch % BOOT_SLOTS], 16 * (batch // BOOT_SLOTS + 1))
                    scale_slab(part, k, boot[batch % BOOT_SLOTS][:, n % BOOT_BATCH, :], sums)
                if part == 2:
                    break
                act.wait_ge(x_in, 16)
                squares()
            split_hi(0, 0, GU_CHUNK)
            uu = 0
            for s in range(N_STAGE):
                for k in range(KD):
                    modulated_hi(s, k)
                kind = stage_kind(s)
                if kind == "F":
                    if kv_sent[s]:
                        act.wait_ge(kv_out, kv_sent[s])
                    for q in range(4):
                        gu_step(s, q, q % 2, GU_CHUNK, first_part(s), SLABS[q])
                    if n_parts(s) > 1:
                        with act.Fori(1, n_parts(s)) as i:
                            for q in range(4):
                                gu_step(s, 4 * i + q, q % 2, GU_CHUNK, first_part(s) + i, SLABS[q])
                    if 2 * n_parts(s) < (GU_STEPS - 2) // 2:
                        with act.Fori(2 * n_parts(s), (GU_STEPS - 2) // 2) as pair:
                            i = 2 * pair
                            for par in range(2):
                                gu_step(s, i + par, par, GU_CHUNK)
                    gu_step(s, GU_STEPS - 2, 0, GU_CHUNK)
                    act.wait_ge(slab_added, added_to(first_part(s) + n_parts(s) - 1, KD - 1))
                    gu_step(s, GU_STEPS - 1, 1, DN_CHUNK)
                    with act.Fori(0, (DN_STEPS - 2) // 2) as pair:
                        i = 2 * pair
                        for par in range(2):
                            dn_step(s, i + par, par, DN_CHUNK)
                    dn_step(s, DN_STEPS - 2, 0, DN_CHUNK)
                    dn_step(s, DN_STEPS - 1, 1, width(s, GU_STEPS + DN_STEPS))
                    continue
                n_g, n_u, nd = GROUPS[kind], len(units(kind)), n_down[kind]

                def split_chunk(c):
                    if width(s, c):
                        split_hi(CB[s] + c - c % 2, c % 2, width(s, c))

                if kind == "C":
                    compress(s)
                split_chunk(nd + 1)
                raw(s, 0)
                qk_copies(s, 0)
                for g in range(n_g):
                    if g + 1 < n_g:
                        split_chunk(nd + g + 2)
                        raw(s, g + 1)
                    for u in range(n_u + 2):
                        if u < n_u:
                            probabilities(s, g, u, uu + u)
                        if u >= 2:
                            p_copy(s, g, u - 2, uu + u - 2)
                    uu += n_u
                    if g + 1 < n_g:
                        qk_copies(s, g + 1)
                    o_hi(s, g)
                for c in range(WO_STEPS):
                    split_chunk(nd + n_g + c + 1)
                    for b in range(2):
                        square(s, 2 * c + b, b)

        @block.vector
        def _(dve):
            chain = Chain(dve, dve_step)
            for c in (w_split_lo, prod_ready, act_ready, x_updated):
                dve.sem_inc(c.sem, 2)
            dve.sem_inc(ssq_ready.sem, 1)

            def split_lo(n, par, w):
                dve.wait_ge(w_split_hi.sem, n + par + 1)
                dve.tensor_tensor(w_lo[par][:, 0:w], w_raw[par][:, 0:w], w_hi[par][:, 0:w],
                                  ALU.subtract).then_inc(w_split_lo.sem, 1)

            def modulation(part, n):
                m = mod[:, part % N_PART * KD:(part % N_PART + n) * KD, :]
                chain.link(dve.tensor_tensor(m, m, mod_b[:, part * KD:(part + n) * KD].unsqueeze(2).to_broadcast(
                    [P, n * KD, 2]), ALU.add))
                for i in range(n):
                    q = (part + i) // 3
                    z = m[:, i * KD:(i + 1) * KD, :]
                    if (part + i) % 3 == 1:
                        chain.link(dve.scalar_tensor_tensor(out=z, in0=z, scalar=1.0,
                                                            in1=gains[:, q, :].unsqueeze(2).to_broadcast([P, KD, 2]),
                                                            op0=ALU.add, op1=ALU.mult))
                    if (part + i) % 3 == 2 and stage_kind(q) == "F":
                        chain.link(dve.tensor_scalar(z, z, FFN_RES, None, ALU.mult))

            def sum_slab(part, k, w, sums, kinds=(1,)):
                if k > 0:
                    dve.wait_ge(slab_summed, summed_to(part, k - 1))
                elif not isinstance(part, int) or part > 0:
                    dve.wait_ge(part_turned, part)
                for c in kinds:
                    if k == 0:
                        ins = dve.tensor_scalar(sums[:, c, :], w, cond[:, k, c:c + 1], None, ALU.mult)
                    else:
                        ins = dve.scalar_tensor_tensor(out=sums[:, c, :], in0=w, scalar=cond[:, k, c:c + 1],
                                                       in1=sums[:, c, :], op0=ALU.mult, op1=ALU.add)
                ins.then_inc(slab_summed, 1)

            def sum_partitions(part, at):
                dve.wait_ge(part_turned, part + 1)
                dve.tensor_reduce(mod[:, bass.ds(at * KD, KD), :].rearrange("p m c -> p c m"),
                                  ps[:, B_PART:B_PART + 4, :].rearrange("p b (m r) -> p (b m) r", r=P).rearrange(
                                      "p (c m) r -> p c m r", c=2), AX.X, ALU.add).then_inc(part_read, 1)

            def norm(s):
                dve.wait_ge(stats_made.sem, stats_made.after(s))
                dve.tensor_scalar(msq[:, 0:TT], ps[:, B_NORM, 0:TT], 1.0 / D, RMS_EPS, ALU.mult,
                                  ALU.add).then_inc(ms_ready.sem, 1)
                dve.wait_ge(rstd_ready.sem, rstd_ready.after(s))
                dve.tensor_tensor(diag[:], ident[:].unsqueeze(1).to_broadcast([P, TT, P]),
                                  rstd[:, 0:TT].unsqueeze(2).to_broadcast([P, TT, P]),
                                  ALU.mult).then_inc(diag_ready.sem, 1)
                dve.wait_ge(rbc_made.sem, rbc_made.after(s))
                m = mod[:, 3 * KD * (s % 3):3 * KD * (s % 3 + 1), :]

                def low(k):
                    dve.wait_ge(h_hi_ready.sem, h_hi_ready.after(s, k))
                    for c, (i, j) in enumerate(((0, P), (P, N_TOK))):
                        ins = dve.scalar_tensor_tensor(out=h_lo[:, k, i:j], in0=tmp[k % 2][:, i:j],
                                                       scalar=m[:, k, c:c + 1], in1=h_hi[:, k, i:j],
                                                       op0=ALU.add, op1=ALU.subtract)
                    ins.then_inc(h_ready.sem, 1)

                for k in range(KD):
                    if k >= 2:
                        low(k - 2)
                        dve.wait_ge(h_ready.sem, h_ready.after(s, k - 2))
                    for c, (i, j) in enumerate(((0, P), (P, N_TOK))):
                        ins = dve.scalar_tensor_tensor(out=tmp[k % 2][:, i:j], in0=x[:, k, i:j],
                                                       scalar=m[:, KD + k, c:c + 1], in1=ps[:, B_NORM, i:j],
                                                       op0=ALU.mult, op1=ALU.mult)
                    ins.then_inc(xr_ready.sem, 1)
                low(KD - 2)
                low(KD - 1)

            def add_squares(s, m, par):
                dve.wait_ge(sq_ready.sem, sq_ready.after(s, m))
                dve.wait_ge(ssq_ready.sem, ssq_ready.at[s] + m)
                dve.tensor_tensor(ssq[:], ssq[:], sq[par][:], ALU.add).then_inc(ssq_ready.sem, 1)

            def residual(s, m, bank, done, val):
                dve.wait_ge(done, val)
                g = mod[:, 3 * KD * (s % 3):3 * KD * (s % 3 + 1), :]
                for c, (i, j) in enumerate(((0, P), (P, N_TOK))):
                    if isinstance(m, int):
                        xs, gate = x[:, m, i:j], g[:, 2 * KD + m, c:c + 1]
                    else:
                        xs = x[:, bass.ds(m, 1), i:j].rearrange("p o t -> p (o t)")
                        gate = g[:, bass.ds(2 * KD + m, 1), c:c + 1].rearrange("p o c -> p (o c)")
                    ins = dve.scalar_tensor_tensor(out=xs, in0=ps[:, bank, i:j], scalar=gate, in1=xs,
                                                   op0=ALU.mult, op1=ALU.add)
                ins.then_inc(x_updated.sem, 1)

            def gu_step(s, j, par, w_next, part=None, slabs=()):
                def sum_next(ks):
                    for k in ks:
                        dve.wait_ge(slab_scaled, scaled_to(part, k))
                        sum_slab(part, k, slab[k % SLAB_SLOTS], acc)

                split_lo(CB[s] + j + 1 - (1 - par), 1 - par, w_next)
                sum_next(slabs[0:2])
                dve.wait_ge(silu_ready.sem, silu_ready.after(s, j))
                dve.wait_ge(act_ready.sem, act_ready.at[s] + j - 1)
                dve.tensor_tensor(prod[par][:], ps[:, 2 * par + 1, 0:N_TOK], sil[par][:],
                                  ALU.mult).then_inc(prod_ready.sem, 1)
                dve.wait_ge(act_hi_ready.sem, act_hi_ready.after(s, j))
                cols = bass.ds(j * N_TOK, N_TOK)
                dve.tensor_tensor(act_lo[:, cols], prod[par][:], act_hi[:, cols],
                                  ALU.subtract).then_inc(act_ready.sem, 1)
                sum_next(slabs[2:])

            def dn_step(s, m, par, w_next):
                if w_next:
                    split_lo(CB[s] + GU_STEPS + m + 1 - (1 - par), 1 - par, w_next)
                residual(s, m, par, w_used.sem, w_used.after(s, GU_STEPS + m))
                add_squares(s, m, par)

            def clear_squares(s):
                dve.wait_ge(rbc_made.sem, rbc_made.after(s))
                chain.link(dve.memset(ssq[:], 0.0))

            def mixer_constants(s):
                kind = stage_kind(s)
                v = tiles[kind]
                dve.wait_ge(mixer_in, n_loads[kind])
                if kind in "AB":
                    nh = HPG[kind] + KVPG[kind]
                    g4 = v["g"].rearrange("p (h e two) -> p h e two", h=nh, two=2)
                    for t in range(2):
                        cos = v["cos"][:, t, :].unsqueeze(1).to_broadcast([P, nh, HD])
                        chain.link(dve.tensor_tensor(v["cg"][:, t, :].rearrange("p (h d) -> p h d", h=nh),
                                                     v["g"].rearrange("p (h d) -> p h d", h=nh), cos, ALU.mult))
                        for e in range(2):
                            sg = v["sg"][:, t, :].rearrange("p (h e two) -> p h e two", h=nh, two=2)[:, :, :, e]
                            sin = v["sin"][:, t, :].rearrange("p (e two) -> p e two", two=2)[:, :, e]
                            chain.link(dve.tensor_tensor(sg, g4[:, :, :, 1 - e],
                                                         sin.unsqueeze(1).to_broadcast([P, nh, HD // 2]), ALU.mult))
                if kind == "A":
                    chain.link(dve.tensor_scalar(v["sink8"][:], v["sink"][:], 1 / scale_of["A"], None, ALU.mult))

            def head_norm(s, g):
                kind = stage_kind(s)
                v = tiles[kind]
                dve.wait_ge(rsq_ready.sem, rsq_ready.after((s, g)))
                if kind == "C":
                    regions = ((slice(0, TT), slice(0, 2), 6, 0), (slice(0, 4), slice(2, 4), 8, 6))
                    for t, h, n, at in regions:
                        chain.link(dve.tensor_reduce(v["hms"][:, at:at + n].rearrange("p (t h) -> p t h", h=2),
                                                     v["sqc"][:, t, h, :], AX.X, ALU.add))
                    dve.tensor_scalar(v["hms"][:, 0:14], v["hms"][:, 0:14], 1.0 / C_QK, RMS_EPS, ALU.mult,
                                      ALU.add).then_inc(hms_ready.sem, 1)
                    yield
                    dve.wait_ge(hrs_ready.sem, hrs_ready.after((s, g)))
                    for i, (t, h, n, at) in enumerate(regions):
                        r = v["hrs"][:, at:at + n].rearrange("p (t h) -> p t h", h=2).unsqueeze(3)
                        z = v["cat"][:, t, h, :]
                        chain.link(dve.tensor_tensor(z, z, r.to_broadcast([P, n // 2, 2, C_QK]), ALU.mult))
                        gain = v["g"][:, i, :].unsqueeze(1).unsqueeze(1).to_broadcast([P, n // 2, 2, C_QK])
                        chain.link(dve.tensor_tensor(z, z, gain, ALU.mult))
                        yield
                    for t in (1, 2):
                        z = v["cat"][:, t, :, C_NOPE:C_QK]
                        z2 = z.rearrange("p h (e two) -> p h e two", two=2)
                        r = v["rope"][:, t - 1]
                        r2 = r.rearrange("p h (e two) -> p h e two", two=2)
                        sin = v["sin"][:, t - 1, :].rearrange("p (e two) -> p e two", two=2)
                        for e in range(2):
                            dve.tensor_tensor(r2[:, :, :, e], z2[:, :, :, 1 - e],
                                              sin[:, :, e].unsqueeze(1).to_broadcast([P, 4, C_ROPE // 2]),
                                              ALU.mult).then_inc(dve_step, 1)
                            chain.local += 1
                        dve.wait_ge(dve_step, chain.value())
                        chain.link(dve.tensor_tensor(z, z, v["cos"][:, t - 1, :].unsqueeze(1).to_broadcast(
                            [P, 4, C_ROPE]), ALU.mult))
                        ins = dve.tensor_tensor(z, z, r, ALU.add)
                        if t == 1:
                            chain.link(ins)
                        else:
                            ins.then_inc(qn_ready.sem, 1)
                        yield
                    return
                nh = HPG[kind] + KVPG[kind]
                hms = v["hms"][:, 0:TT * nh]
                nrm = v["nrm"].rearrange("p t (h d) -> p t h d", h=nh)
                chain.link(dve.tensor_reduce(hms.rearrange("p (t h) -> p t h", h=nh), nrm, AX.X, ALU.add))
                dve.tensor_scalar(hms, hms, 1.0 / HD, RMS_EPS, ALU.mult, ALU.add).then_inc(hms_ready.sem, 1)
                yield
                dve.wait_ge(hrs_ready.sem, hrs_ready.after((s, g)))
                raw = v["raw"][g % 2][:, :, 0:nh * HD].rearrange("p t (h d) -> p t h d", h=nh)
                r = v["hrs"][:, 0:TT * nh].rearrange("p (t h) -> p t h", h=nh).unsqueeze(3)
                chain.link(dve.tensor_tensor(nrm, raw, r.to_broadcast([P, TT, nh, HD]), ALU.mult))
                yield
                if g >= 1:
                    dve.wait_ge(kv_out, kv_sent[s, g - 1])
                qn = v["qn"]
                if kind == "D":
                    dve.tensor_tensor(qn[:], v["nrm"][:], v["g"][:].unsqueeze(1).to_broadcast([P, TT, nh * HD]),
                                      ALU.mult).then_inc(qn_ready.sem, 1)
                    yield
                    return
                chain.link(dve.tensor_tensor(qn[:, 0, 0:nh * HD], v["nrm"][:, 0, :], v["g"][:], ALU.mult))
                lat = v["nrm"][:, 1:3, :]
                pair = "p t (e two) -> p t e two"
                for e in range(2):
                    chain.link(dve.tensor_tensor(v["rope"].rearrange(pair, two=2)[:, :, :, e],
                                                 lat.rearrange(pair, two=2)[:, :, :, 1 - e],
                                                 v["sg"].rearrange(pair, two=2)[:, :, :, e], ALU.mult))
                yield
                chain.link(dve.tensor_tensor(lat, lat, v["cg"][:], ALU.mult))
                yield
                chain.link(dve.tensor_tensor(qn[:, 1:3, 0:nh * HD], lat, v["rope"][:], ALU.add))
                dve.tensor_copy(qn[:, :, nh * HD:(nh + 1) * HD], qn[:, :, (nh - 1) * HD:nh * HD]
                                ).then_inc(qn_ready.sem, 1)
                yield

            def head_bias(s, g):
                v = tiles["D"]
                dve.wait_ge(bias_in[g % 2], 64 * (g // 2 + 1))
                b = v["bias"][g % 2].rearrange("p h d c -> p (h d) c")
                chain.link(dve.scalar_tensor_tensor(out=b, in0=b, scalar=1 / scale_of["D"],
                                                    in1=v["mask"][:].unsqueeze(1).to_broadcast([P, 12, GRID_W]),
                                                    op0=ALU.mult, op1=ALU.add))

            def maximum(s, g, u, uu):
                kind = stage_kind(s)
                v = tiles[kind]
                what, h, t = units(kind)[u]
                bank, st = B_S[uu % 3], v["stat"]
                dve.wait_ge(s_made.sem, s_made.after((s, g, u)))
                n = HPG[kind] if what == "ctx" else 1
                w = P if what == "ctx" else N_LAT + N_PAST
                if kind == "A" and what == "lat":
                    blk = ps[:, bank, (2 - t) * P:(3 - t) * P]
                    chain.link(dve.tensor_tensor(blk, blk, v["mask"][:, t - 1, :], ALU.add))
                if kind == "D" and what == "lat":
                    blk = ps[:, bank, 0:N_LAT].rearrange("p (r c) -> p r c", c=GRID_W)
                    d0 = 4 - 2 * t
                    b = v["bias"][g % 2][:, h, d0:d0 + GRID_H, :]
                    rev = bass.AP(tensor=b.tensor, offset=b.offset + GRID_W - 1,
                                  ap=[list(b.ap[0]), [GRID_W, GRID_H], [-1, GRID_W]])
                    chain.link(dve.tensor_tensor(blk, blk, rev, ALU.add))
                chain.link(dve.tensor_reduce(st[:, uu % 3, 0, 0:n],
                                             ps[:, bank, 0:n * w].rearrange("p (n w) -> p n w", w=w), AX.X, ALU.max))
                mx, nb = st[:, uu % 3, 0, 0:n], st[:, uu % 3, 1, 0:n]
                if kind != "A":
                    dve.tensor_scalar(nb, mx, -scale_of[kind], None, ALU.mult).then_inc(max_ready.sem, 1)
                    return
                h0 = g * HPG[kind] + (0 if what == "ctx" else h)
                chain.link(dve.tensor_tensor(mx, mx, v["sink8"][:, h0:h0 + n], ALU.max))
                chain.link(dve.tensor_scalar(nb, mx, -scale_of[kind], None, ALU.mult))
                dve.tensor_tensor(st[:, uu % 3, 3, 0:n], v["sink"][:, h0:h0 + n], nb, ALU.add
                                  ).then_inc(max_ready.sem, 1)

            def o_copy(s, g, u, uu):
                kind = stage_kind(s)
                v = tiles[kind]
                what, h, t = units(kind)[u]
                st = v["stat"][:, uu % 3]
                n = HPG[kind] if what == "ctx" else 1
                r = v["rinv"][:, uu % 4, 0:n]
                dve.wait_ge(o_made.sem, o_made.after((s, g, u)))
                o = ps[:, B_O[uu % 2], 0:n * HD].rearrange("p (n d) -> p n d", d=HD)
                at = 0 if what == "ctx" else h * HD
                dst = v["o"][:, t, at:at + n * HD].rearrange("p (n d) -> p n d", d=HD)
                dve.tensor_tensor(dst, o, r.unsqueeze(2).to_broadcast([P, n, HD]), ALU.mult).then_inc(o_ready.sem, 1)

            def inverse(s, g, u, uu):
                kind = stage_kind(s)
                v = tiles[kind]
                what, h, t = units(kind)[u]
                st = v["stat"][:, uu % 3]
                n = HPG[kind] if what == "ctx" else 1
                dve.wait_ge(exp_ready.sem, exp_ready.after((s, g, u)))
                if kind == "A":
                    chain.link(dve.tensor_tensor(st[:, 2, 0:n], st[:, 2, 0:n], st[:, 3, 0:n], ALU.add))
                chain.link(dve.reciprocal(v["rinv"][:, uu % 4, 0:n], st[:, 2, 0:n]))

            def o_lo(s, g):
                kind = stage_kind(s)
                v = tiles[kind]
                dve.wait_ge(ot_hi_ready.sem, ot_hi_ready.after((s, g)))
                for n in range(HPG[kind] // 2):
                    k = g * HPG[kind] // 2 + n
                    ins = dve.tensor_tensor(v["oT_lo"][:, k, :], ps[:, B_O[n], 0:N_TOK], v["oT_hi"][:, k, :],
                                            ALU.subtract)
                ins.then_inc(ot_ready.sem, 1)

            def compress(s):
                v = tiles["C"]
                split_lo(CB[s], 1, width(s, 1))
                split_lo(CB[s] + 2, 0, width(s, 2))
                dve.wait_ge(c_raw_ready, 1)
                for c, n in enumerate((C_Q_RANK, C_KV_RANK)):
                    ins = dve.tensor_scalar(v["cms"][:, c, :], v["cms"][:, c, :], 1.0 / n, RMS_EPS, ALU.mult, ALU.add)
                    if c == 0:
                        chain.link(ins)
                ins.then_inc(c_norm_ready.sem, 1)
                dve.tensor_copy(v["kr"][:, 0:TT, :], v["cdn"][:, :, C_Q_RANK + C_KV_RANK:C_DOWN]
                                ).then_inc(c_norm_ready.sem, 1)
                dve.wait_ge(c_rstd_ready.sem, 1)
                for c, (i, j) in enumerate(((0, C_Q_RANK), (C_Q_RANK, C_Q_RANK + C_KV_RANK))):
                    for t in range(TT):
                        ins = dve.scalar_tensor_tensor(out=v["cdn"][:, t, i:j], in0=v["cdn"][:, t, i:j],
                                                       scalar=v["crs"][:, c, t:t + 1], in1=v["gd"][:, i:j],
                                                       op0=ALU.mult, op1=ALU.mult)
                ins.then_inc(c_norm_ready.sem, 1)
                for n in range(KQ + KC):
                    dve.wait_ge(c_hi_ready, n + 1)
                    hi, lo = ((v["cqT_hi"][:, n, :], v["cqT_lo"][:, n, :]) if n < KQ else
                              (v["ckT_hi"][:, n - KQ, 0:N_TOK], v["ckT_lo"][:, n - KQ, 0:N_TOK]))
                    dve.tensor_tensor(lo, ps[:, CT_BANKS[n], 0:N_TOK], hi, ALU.subtract).then_inc(c_t_ready, 1)
                dve.wait_ge(c_hi_ready, KQ + KC + 1)
                dve.tensor_tensor(v["ckT_lo"][:, :, N_TOK:N_TOK + N_PAST], v["cache"][:],
                                  v["ckT_hi"][:, :, N_TOK:N_TOK + N_PAST], ALU.subtract).then_inc(c_t_ready, 1)

            chain.link(dve.memset(ssq[:], 0.0))
            dve.wait_ge(x_in, 16)
            dve.wait_ge(act_step, 1)
            for part in range(3):
                for k in range(KD):
                    n = part * KD + k
                    batch = n // BOOT_BATCH
                    dve.wait_ge(boot_landed[batch % BOOT_SLOTS], 16 * (batch // BOOT_SLOTS + 1))
                    sum_slab(part, k, boot[batch % BOOT_SLOTS][:, n % BOOT_BATCH, :],
                             acc_of_scale if part == 1 else acc, (0, 1) if part == 0 else (1,))
                if part == 1:
                    sum_partitions(0, 0)
                    for m in range(KD):
                        add_squares(-1, m, m % 2)
            sum_partitions(1, 1)
            sum_partitions(2, 2)
            dve.wait_ge(part_read, 3)
            modulation(0, 3)
            split_lo(0, 0, GU_CHUNK)
            uu = 0
            for s in range(N_STAGE):
                norm(s)
                clear_squares(s)
                kind = stage_kind(s)
                if kind == "F":
                    part, n, at = first_part(s), n_parts(s), first_part(s) % N_PART
                    for q in range(4):
                        gu_step(s, q, q % 2, GU_CHUNK, part, SLABS[q])
                    sum_partitions(part, at)
                    if n > 1:
                        with dve.Fori(1, n) as i:
                            for q in range(4):
                                gu_step(s, 4 * i + q, q % 2, GU_CHUNK, part + i, SLABS[q])
                            sum_partitions(part + i, i + 3 if at == 3 else i - 1)
                    if 2 * n < (GU_STEPS - 2) // 2:
                        with dve.Fori(2 * n, (GU_STEPS - 2) // 2) as pair:
                            i = 2 * pair
                            for par in range(2):
                                gu_step(s, i + par, par, GU_CHUNK)
                    gu_step(s, GU_STEPS - 2, 0, GU_CHUNK)
                    gu_step(s, GU_STEPS - 1, 1, DN_CHUNK)
                    dve.wait_ge(part_read, part + n)
                    if at == 3:
                        modulation(part, n)
                    else:
                        modulation(part, 1)
                        if n > 1:
                            modulation(part + 1, n - 1)
                    with dve.Fori(0, (DN_STEPS - 2) // 2) as pair:
                        i = 2 * pair
                        for par in range(2):
                            dn_step(s, i + par, par, DN_CHUNK)
                    dn_step(s, DN_STEPS - 2, 0, DN_CHUNK)
                    dn_step(s, DN_STEPS - 1, 1, width(s, GU_STEPS + DN_STEPS))
                    continue
                n_g, n_u, nd = GROUPS[kind], len(units(kind)), n_down[kind]

                def split_chunk(c):
                    if width(s, c):
                        split_lo(CB[s] + c - c % 2, c % 2, width(s, c))

                mixer_constants(s)
                if kind == "C":
                    compress(s)
                split_chunk(nd + 1)
                for _ in head_norm(s, 0):
                    pass
                for g in range(n_g):
                    ahead = iter(())
                    if g + 1 < n_g:
                        split_chunk(nd + g + 2)
                        ahead = head_norm(s, g + 1)
                    if kind == "D":
                        head_bias(s, g)
                    for u in range(n_u + 3):
                        if u < n_u:
                            maximum(s, g, u, uu + u)
                        if 1 <= u <= n_u:
                            inverse(s, g, u - 1, uu + u - 1)
                        if u >= 3:
                            o_copy(s, g, u - 3, uu + u - 3)
                        if u >= 1:
                            next(ahead, None)
                    for _ in ahead:
                        pass
                    uu += n_u
                    o_lo(s, g)
                for c in range(WO_STEPS):
                    split_chunk(nd + n_g + c + 1)
                    for b in range(2):
                        m = 2 * c + b
                        if b == 0:
                            residual(s, m, b, wo_half.sem, wo_half.after(s, c))
                        else:
                            residual(s, m, b, w_used.sem, w_used.after(s, nd + n_g + c))
                        add_squares(s, m, b)


def kernel(**inputs):
    import concourse.bacc as bacc
    from concourse.bass_utils import run_bass_kernel_spmd

    def arr(name):
        return np.asarray(inputs[name])

    def rows(w, *shape):
        return w.reshape(w.shape[0] // P, P, *shape)

    def by_channel(w):
        return w.reshape(w.shape[0], -1, P).transpose(2, 0, 1)

    a = {}
    x = np.concatenate([arr("x_prompt")[0], arr("x_sample")[0]], axis=0)
    a["x"] = x.T.reshape(KD, P, N_TOK).transpose(1, 0, 2)
    a["cond"] = np.stack([arr("c_ctx"), arr("c")[0]], axis=-1).reshape(KD, P, 2).transpose(1, 0, 2)
    a["mod_w"] = arr("mod_w").reshape(DEPTH, KD, P, N_PART, D).transpose(0, 3, 1, 2, 4).reshape(-1, P, D)
    a["mod_b"] = arr("mod_b").reshape(-1, P).T
    a["gains"] = by_channel(np.stack([arr("norm_ff1"), arr("norm_mix"), arr("norm_ff2")], axis=1).reshape(N_STAGE, D))
    a["ident"] = np.eye(P, dtype=np.float32)
    gu = np.stack([arr("ff1_w_gu"), arr("ff2_w_gu")], axis=1)
    a["ffn_gu"] = gu.reshape(2 * DEPTH, KD, P, 2, KF, P).transpose(0, 4, 2, 1, 3, 5).reshape(-1, P, GU_CHUNK)
    dn = np.stack([arr("ff1_w_down"), arr("ff2_w_down")], axis=1)
    a["ffn_dn"] = dn.reshape(2 * DEPTH, KF, P, KD, P).transpose(0, 3, 2, 1, 4).reshape(-1, P, DN_CHUNK)

    def wo(w):
        return w.reshape(KD, P, WO_STEPS, 2 * P).transpose(2, 1, 0, 3).reshape(WO_STEPS, P, WO_CHUNK)

    def qkv(w, heads, kv_heads, groups):
        w = w.reshape(KD, P, -1)
        nq, nk = heads * HD, kv_heads * HD
        parts = [w[:, :, i:i + n].reshape(KD, P, groups, n // groups)
                 for i, n in ((0, nq), (nq, nk), (nq + nk, nk))]
        return np.concatenate(parts, axis=3).transpose(2, 1, 0, 3).reshape(groups, P, QKV_CHUNK)

    pos = np.arange(N_LAT)

    def rope(dim):
        n = dim // 4
        inv = np.float32(ROPE_THETA) ** (-np.arange(n, dtype=np.float32) / np.float32(n))
        ang = np.concatenate([(pos // GRID_W).astype(np.float32)[:, None] * inv,
                              (pos % GRID_W).astype(np.float32)[:, None] * inv], axis=-1)
        c, s = np.cos(ang), np.sin(ang)
        c, s = np.stack([c, c], axis=-1), np.stack([-s, s], axis=-1)
        return [z.reshape(2, P, dim).transpose(1, 0, 2) for z in (c, s)]

    def everywhere(v):
        return np.broadcast_to(v, (P, *v.shape))

    for kind in "ab":
        a[f"{kind}_w"] = qkv(arr(f"{kind}_w_qkv")[0], HEADS, KV_HEADS, 4)
        a[f"{kind}_wo"] = wo(arr(f"{kind}_w_o")[0])
        a[f"{kind}_g"] = everywhere(np.concatenate([arr(f"{kind}_q_norm")[0]] * 4 + [arr(f"{kind}_k_norm")[0]]))
        a[f"{kind}_cos"], a[f"{kind}_sin"] = rope(HD)
        ck = arr(f"cache_{kind}_k")[0, 0].transpose(2, 1, 0)
        a[f"{kind}_ck"] = np.concatenate([ck, ck], axis=0)
        a[f"{kind}_cv"] = arr(f"cache_{kind}_v")[0, 0].reshape(N_PAST, KV_HEADS * HD)
    q, k = pos[:, None], pos[None, :]
    outside = np.where(np.abs(q - k) <= A_WINDOW, np.float32(0), np.float32(NEG))
    a["a_mask"] = np.stack([outside[0:P, P:], outside[P:, 0:P]], axis=1)
    a["a_sink"] = everywhere(arr("a_sink")[0])

    dn = arr("c_w_down")[0].reshape(KD, P, C_DOWN).transpose(1, 0, 2)
    a["c_dn0"] = dn[:, :, 0:C_Q_RANK].reshape(P, -1)
    a["c_dn1"] = dn[:, :, C_Q_RANK:].reshape(P, -1)
    uq = arr("c_w_uq")[0].reshape(KQ, P, 8, C_UQ_W).transpose(2, 1, 0, 3).reshape(8, P, -1)
    ukv = arr("c_w_ukv")[0].reshape(KC, P, 8, C_UKV_W).transpose(2, 1, 0, 3).reshape(8, P, -1)
    a["c_w"] = np.concatenate([uq, ukv], axis=2)
    a["c_wo"] = wo(arr("c_w_o")[0])
    a["c_g"] = everywhere(np.stack([arr("c_q_norm")[0], arr("c_k_norm")[0]]))
    a["c_gd"] = everywhere(np.concatenate([arr("c_q_lnorm")[0], arr("c_kv_lnorm")[0]]))
    a["c_cos"], a["c_sin"] = rope(C_ROPE)
    a["c_cache"] = arr("cache_c_kv")[0, 0].T.reshape(KC, P, N_PAST).transpose(1, 0, 2)
    a["c_kr"] = arr("cache_c_krope")[0, 0]

    a["d_w"] = qkv(arr("d_w_qkv")[0], HEADS, HEADS, 8)
    a["d_wo"] = wo(arr("d_w_o")[0])
    a["d_g"] = everywhere(np.concatenate([arr("d_q_norm")[0]] * 2 + [arr("d_k_norm")[0]] * 2))
    a["d_ck"] = arr("cache_d_k")[0, 0].transpose(1, 2, 0).reshape(8, P, N_PAST).transpose(1, 0, 2)
    a["d_cv"] = arr("cache_d_v")[0, 0].reshape(N_PAST, HEADS * HD)
    rpb = np.zeros((HEADS, RPB_R, RPB_W), np.float32)
    rpb[:, :, RPB_PAD:RPB_PAD + RPB_C] = arr("d_rpb")[0, :, :, ::-1]
    a["d_rpb"] = rpb
    qc, kc = np.arange(GRID_W)[:, None], np.arange(GRID_W)[None, ::-1]
    first = np.clip(qc - NA_COLS // 2, 0, GRID_W - NA_COLS)
    inside = np.where((kc >= first) & (kc < first + NA_COLS), np.float32(0), np.float32(NEG))
    a["d_mask"] = np.concatenate([inside, inside], axis=0)

    outs = {"y": (P, KD, N_TOK), "new_a_k": (P, KV_HEADS * HD), "new_a_v": (P, KV_HEADS * HD),
            "new_b_k": (P, KV_HEADS * HD), "new_b_v": (P, KV_HEADS * HD),
            "new_c_kv": (P, C_KV_RANK), "new_c_krope": (P, C_ROPE),
            "new_d_k": (P, HEADS * HD), "new_d_v": (P, HEADS * HD)}
    nc = bacc.Bacc("TRN2", target_bir_lowering=False, num_devices=1)
    arrays, ins = {}, {}
    for name, v in a.items():
        v = np.ascontiguousarray(v)
        arrays[f"in_{name}"] = v
        ins[name] = nc.dram_tensor(f"in_{name}", v.shape, F32, kind="ExternalInput").ap()
    outputs = {name: nc.dram_tensor(f"out_{name}", shape, F32, kind="ExternalOutput").ap()
               for name, shape in outs.items()}
    build(nc, ins, outputs)
    got = run_bass_kernel_spmd(nc, [arrays], core_ids=[0]).results[0]
    r = {name: np.asarray(got[f"out_{name}"]) for name in outs}
    y = r["y"].transpose(1, 0, 2).reshape(D, N_TOK).T
    return (y[0:N_CTX][None], y[N_CTX:][None],
            r["new_a_k"].reshape(1, 1, P, KV_HEADS, HD), r["new_a_v"].reshape(1, 1, P, KV_HEADS, HD),
            r["new_b_k"].reshape(1, 1, P, KV_HEADS, HD), r["new_b_v"].reshape(1, 1, P, KV_HEADS, HD),
            r["new_c_kv"].reshape(1, 1, P, C_KV_RANK), r["new_c_krope"].reshape(1, 1, P, C_ROPE),
            r["new_d_k"].reshape(1, 1, P, HEADS, HD), r["new_d_v"].reshape(1, 1, P, HEADS, HD))
```

```python
from contextlib import ExitStack

import numpy as np

import concourse.bass as bass
from concourse import mybir

ALU = mybir.AluOpType
ACT = mybir.ActivationFunctionType
AX = mybir.AxisListType
F32 = mybir.dt.float32
F32R = mybir.dt.float32r

P = 128
D = 1024
KD = D // P
N_CTX = 128
N_LAT = 256
N_TOK = N_CTX + N_LAT
TT = N_TOK // P
N_PAST = 128
D_FF = 2816
KF = D_FF // P
DEPTH = 4
N_STAGE = 3 * DEPTH
HD = 64
HEADS = 16
KV_HEADS = 4
GRID_W = 64
GRID_H = N_LAT // GRID_W
A_WINDOW = 128
C_Q_RANK, C_KV_RANK, C_ROPE, C_NOPE = 384, 256, 32, 64
KQ, KC = C_Q_RANK // P, C_KV_RANK // P
C_QK = C_NOPE + C_ROPE
C_DOWN = C_Q_RANK + C_KV_RANK + C_ROPE
NA_ROWS, NA_COLS = 8, 16
RPB_R, RPB_C = 2 * NA_ROWS - 1, 2 * NA_COLS - 1
RPB_PAD = GRID_W - NA_COLS
RPB_W = RPB_C + 2 * RPB_PAD
RMS_EPS = 1e-6
ROPE_THETA = 10000.0
NEG = -1e30
FFN_RES = 0.5

GU_STEPS = KF
GU_CHUNK = KD * 2 * P
DN_STEPS = KD
DN_CHUNK = KF * P
WO_STEPS = KD // 2
WO_CHUNK = KD * 2 * P
QKV_W = 384
QKV_CHUNK = KD * QKV_W
QKT_BANKS = (2, 4, 0, 1)
C_BANKS = ((0, 1, 2), (3, 6, 7))
CT_BANKS = (0, 1, 2, 3, 5)
C_DOWN_COLS = (C_Q_RANK, C_KV_RANK + C_ROPE)
C_UQ_W, C_UKV_W = 2 * C_QK, 2 * 2 * HD
C_UP_CHUNK = KQ * C_UQ_W + KC * C_UKV_W
SLOT = QKV_CHUNK

N_PART = 9
SLABS = ((0, 1), (2, 3, 4), (5, 6, 7), ())
SLAB_SLOTS = 4
BOOT_BATCH, BOOT_SLOTS = 2, 8
BOOT_FLIGHT = 3


B_NORM = 3
B_PART = 4
B_S = (0, 1)
B_P = (2, 4)
B_O = (3, 5)
B_PT = (6, 7)
GROUPS = {"A": 4, "B": 4, "C": 8, "D": 8}
HPG = {"A": 4, "B": 4, "C": 2, "D": 2}
KVPG = {"A": 1, "B": 1, "C": 2, "D": 2}


def stage_kind(s):
    return "ABCD"[(s // 3) % 4] if s % 3 == 1 else "F"


def chunk_base():
    per = {"F": GU_STEPS + DN_STEPS, "A": 4 + WO_STEPS, "B": 4 + WO_STEPS,
           "C": 2 + 8 + WO_STEPS, "D": 8 + WO_STEPS}
    base = [0]
    for s in range(N_STAGE):
        assert base[-1] % 2 == 0
        base.append(base[-1] + per[stage_kind(s)])
    return base


CB = chunk_base()


def first_part(s):
    return N_PART * (s // 3) + (3 if s % 3 == 0 else 8)


def n_parts(s):
    return 5 if s % 3 == 0 else 4 if s + 1 < N_STAGE else 1



def proj_tiles(kind):
    return 4 if kind == "C" else TT


def out_bank(kind, g, pair):
    return B_O[pair if HPG[kind] > 2 else g % 2]


def proj_bank(g, t):
    return t if g == 0 else B_P[t % 2]


def units(kind):
    return [("ctx", None, 0)] + [("lat", h, t) for h in range(HPG[kind]) for t in (1, 2)]


class Count:

    def __init__(self, sem, start=0):
        self.sem, self.n, self.at = sem, start, {}

    def mark(self, key, times=1):
        self.at[key] = self.n
        self.n += times

    def after(self, key, i=0):
        return self.at[key] + i + 1


class Chain:

    def __init__(self, eng, s):
        self.eng, self.sem, self.base, self.per, self.i, self.local = eng, s, 0, 0, None, 0

    def value(self):
        v = self.base + self.local
        return v if self.i is None else v + self.i * self.per

    def link(self, ins):
        ins.then_inc(self.sem, 1)
        self.local += 1
        self.eng.wait_ge(self.sem, self.value())

    def enter(self, i, per):
        self.base, self.local, self.i, self.per = self.base + self.local, 0, i, per

    def leave(self, rounds):
        assert self.local == self.per, (self.local, self.per)
        self.base, self.local, self.i, self.per = self.base + rounds * self.per, 0, None, 0


def qkt_types(kind):
    if kind in "AB":
        return [("q", 0, P), ("q", 1, P), ("k", 0, P)]
    if kind == "D":
        return [("q", 0, P), ("k", 0, P)]
    return [("q", 0, C_QK), ("q", 1, C_QK), ("k", 0, C_QK), ("k", 1, C_QK)]


def build(nc, a, out):
    with ExitStack() as ctx:
        def sb(name, shape, dt=F32):
            return ctx.enter_context(nc.sbuf_tensor(name, shape, dt))[:]

        def sem(name):
            return ctx.enter_context(nc.semaphore(name))

        ps = ctx.enter_context(nc.psum_tensor("ps", [P, 8, 512], F32))[:]

        x = sb("x", [P, KD, N_TOK])
        h_hi = sb("h_hi", [P, KD, N_TOK], F32R)
        h_lo = sb("h_lo", [P, KD, N_TOK], F32R)
        w_raw = [sb(f"w_raw{i}", [P, SLOT]) for i in range(2)]
        w_hi, scaled = [], []
        for i in range(2):
            with ExitStack() as tail:
                tail.enter_context(nc.sbuf_tensor(f"w_hi{i}_chunk", [P, GU_CHUNK], F32R))
                scaled.append(tail.enter_context(nc.sbuf_tensor(f"scaled{i}", [P, D], F32))[:])
            w_hi.append(sb(f"w_hi{i}", [P, SLOT], F32R))
        w_lo = [sb(f"w_lo{i}", [P, SLOT], F32R) for i in range(2)]
        slab = [sb(f"slab{i}", [P, D]) for i in range(2)] + [w[:, GU_CHUNK:GU_CHUNK + D] for w in w_raw]
        ident = sb("ident", [P, P])
        ones = sb("ones", [P, P])
        neghalf = sb("neghalf", [P, 16])
        cond = sb("cond", [P, KD, 2])
        mod_b = sb("mod_b", [P, DEPTH * N_PART * KD])
        gains = sb("gains", [P, N_STAGE, KD])
        mod = sb("mod", [P, N_PART * KD, 2])
        ssq = sb("ssq", [P, N_TOK])
        sq = [sb(f"sq{i}", [P, N_TOK]) for i in range(2)]
        rstd = sb("rstd", [P, 4])
        msq = sb("msq", [P, 4])
        diag = sb("diag", [P, TT, P])
        tmp = [sb(f"tmp{i}", [P, N_TOK]) for i in range(2)]

        cond_in = sem("cond_in")
        x_in = sem("x_in")
        consts_in = sem("consts_in")
        w_landed = [sem("w_landed0"), sem("w_landed1")]
        slab_landed = [sem(f"slab_landed{i}") for i in range(SLAB_SLOTS)]
        boot_landed = [sem(f"boot_landed{i}") for i in range(BOOT_SLOTS)]
        mixer_in = sem("mixer_in")
        w_split_hi = Count(sem("w_split_hi"))
        w_split_lo = Count(sem("w_split_lo"), 2)
        w_used = Count(sem("w_used"), 2)
        slab_scaled = sem("slab_scaled")
        slab_added = sem("slab_added")
        slab_summed = sem("slab_summed")
        part_turned = sem("part_turned")
        part_read = sem("part_read")
        act_ready = Count(sem("act_ready"), 2)
        x_updated = Count(sem("x_updated"), 2)
        sq_ready = Count(sem("sq_ready"))
        ssq_ready = Count(sem("ssq_ready"), 1)
        silu_ready = Count(sem("silu_ready"))
        act_hi_ready = Count(sem("act_hi_ready"))
        prod_ready = Count(sem("prod_ready"), 2)
        stats_made = Count(sem("stats_made"))
        ms_ready = Count(sem("ms_ready"))
        rstd_ready = Count(sem("rstd_ready"))
        diag_ready = Count(sem("diag_ready"))
        rbc_made = Count(sem("rbc_made"))
        xr_ready = Count(sem("xr_ready"))
        h_hi_ready = Count(sem("h_hi_ready"))
        h_ready = Count(sem("h_ready"))
        proj_made = Count(sem("proj_made"))
        raw_ready = Count(sem("raw_ready"))
        rsq_ready = Count(sem("rsq_ready"))
        hms_ready = Count(sem("hms_ready"))
        hrs_ready = Count(sem("hrs_ready"))
        head_scaled = Count(sem("head_scaled"))
        qn_ready = Count(sem("qn_ready"))
        qkt_made = Count(sem("qkt_made"))
        qkt_ready = Count(sem("qkt_ready"))
        s_made = Count(sem("s_made"))
        max_ready = Count(sem("max_ready"))
        exp_ready = Count(sem("exp_ready"))
        p_scaled = Count(sem("p_scaled"))
        pt_made = Count(sem("pt_made"))
        pt_ready = Count(sem("pt_ready"))
        o_made = Count(sem("o_made"))
        ot_hi_ready = Count(sem("ot_hi_ready"))
        ot_ready = Count(sem("ot_ready"))
        wo_half = Count(sem("wo_half"))
        c_raw_ready = sem("c_raw_ready")
        c_rstd_ready = Count(sem("c_rstd_ready"))
        kr_ready = Count(sem("kr_ready"))
        c_norm_ready = Count(sem("c_norm_ready"))
        c_t_made = sem("c_t_made")
        c_hi_ready = sem("c_hi_ready")
        c_t_ready = sem("c_t_ready")
        bias_in = [sem("bias_in0"), sem("bias_in1")]
        out_done = sem("out_done")
        kv_out = sem("kv_out")
        pe_step, act_step, dve_step, pool_step = (sem(n) for n in ("pe_step", "act_step", "dve_step", "pool_step"))

        first_unit, kv_sent, n_kv = {}, {}, 0
        sq_ready.mark(-1, KD)
        ssq_ready.mark(-1, KD)
        for s in range(N_STAGE):
            kind = stage_kind(s)
            n_chunks = CB[s + 1] - CB[s]
            w_split_hi.mark(s, n_chunks)
            w_split_lo.mark(s, n_chunks)
            w_used.mark(s, n_chunks)
            if kind == "F":
                for c in (act_ready, silu_ready, act_hi_ready, prod_ready):
                    c.mark(s, GU_STEPS)
            else:
                first_unit[s] = s_made.n
                if kind == "C":
                    for key in ("ms", "kr", "cq"):
                        c_norm_ready.mark(key)
                    c_rstd_ready.mark("ms")
                for g in range(GROUPS[kind]):
                    if kind == "C":
                        kr_ready.mark((s, g))
                    proj_made.mark((s, g), proj_tiles(kind) - 1)
                    raw_ready.mark((s, g), proj_tiles(kind))
                    rsq_ready.mark((s, g))
                    hms_ready.mark((s, g))
                    hrs_ready.mark((s, g))
                    head_scaled.mark((s, g))
                    qn_ready.mark((s, g))
                    types = len(qkt_types(kind))
                    qkt_made.mark((s, g), types)
                    qkt_ready.mark((s, g), types)
                    for u in range(len(units(kind))):
                        for c in (s_made, max_ready, exp_ready, p_scaled, pt_made, pt_ready, o_made):
                            c.mark((s, g, u))
                    ot_hi_ready.mark((s, g))
                    ot_ready.mark((s, g))
                wo_half.mark(s, WO_STEPS)
                for g in range(GROUPS[kind]):
                    n_kv += 32 if kind != "C" or g == 0 else 0
                    kv_sent[s, g] = n_kv
            kv_sent[s] = n_kv
            for c in (x_updated, sq_ready, ssq_ready):
                c.mark(s, KD)
            for c in (ms_ready, rstd_ready, diag_ready, rbc_made, stats_made):
                c.mark(s)
            for c in (xr_ready, h_hi_ready, h_ready):
                c.mark(s, KD)

        tiles = {}
        for kind in "FABCD":
            with ExitStack() as own:
                def part(name, shape, dt=F32):
                    return own.enter_context(nc.sbuf_tensor(f"{kind}_{name}", shape, dt))[:]

                v = tiles[kind] = {}
                if kind == "F":
                    v["acc"] = part("acc", [P, 2, D])
                    with ExitStack() as at_first:
                        v["boot"] = [at_first.enter_context(nc.sbuf_tensor(f"boot{i}", [P, BOOT_BATCH, D], F32))[:]
                                     for i in range(BOOT_SLOTS)]
                    v["act_hi"] = part("act_hi", [P, KF * N_TOK], F32R)
                    v["act_lo"] = part("act_lo", [P, KF * N_TOK], F32R)
                    continue
                w = C_UQ_W + C_UKV_W if kind == "C" else QKV_W
                nh = HPG[kind] + KVPG[kind]
                v["p"] = [part(f"p{i}", [P, 512]) for i in range(3)]
                v["pt"] = [part(f"pt{i}", [P, 512]) for i in range(2)]
                v["stat"] = part("stat", [P, 3, 5, 4])
                v["rinv"] = part("rinv", [P, 4, 4])
                v["hms"] = part("hms", [P, 16])
                v["hrs"] = part("hrs", [P, 16])
                if kind == "C":
                    v["cat"] = [part(f"cat{i}", [P, 4, 4, C_QK]) for i in range(2)]
                    v["sqc"] = part("sqc", [P, 4, 4, C_QK])
                    v["v"] = [part(f"v{i}", [P, 4, 2 * HD]) for i in range(3)]
                    v["cdn"] = part("cdn", [P, TT, C_DOWN])
                    v["kr"] = part("kr", [P, 4, C_ROPE])
                    v["junk"] = part("junk", [P, C_Q_RANK])
                    v["cms"] = part("cms", [P, 2, TT])
                    v["crs"] = part("crs", [P, 2, TT])
                    v["cqT_hi"] = part("cqT_hi", [P, KQ, N_TOK], F32R)
                    v["cqT_lo"] = part("cqT_lo", [P, KQ, N_TOK], F32R)
                    v["ckT_hi"] = part("ckT_hi", [P, KC, N_TOK + N_PAST], F32R)
                    v["ckT_lo"] = part("ckT_lo", [P, KC, N_TOK + N_PAST], F32R)
                    v["cache"] = part("cache", [P, KC, N_PAST])
                    v["gd"] = part("gd", [P, C_Q_RANK + C_KV_RANK])
                    v["g"] = part("g", [P, 2, C_QK])
                    v["cos"] = part("cos", [P, 2, C_ROPE])
                    v["sin"] = part("sin", [P, 2, C_ROPE])
                    v["rope"] = part("rope", [P, 2, 4, C_ROPE])
                    v["qt"] = part("qt", [P, 2, N_TOK])
                    v["kt"] = part("kt", [P, 2, N_TOK + N_PAST])
                    v["oT_hi"], v["oT_lo"] = h_hi, h_lo
                else:
                    v["raw"] = [part(f"raw{i}", [P, TT, QKV_W]) for i in range(3)]
                    v["nrm"] = part("nrm", [P, TT, nh * HD])
                    v["qn"] = part("qn", [P, TT, (HPG[kind] + 2) * HD])
                    v["g"] = part("g", [P, nh * HD])
                    v["qt"] = part("qt", [P, HPG[kind] // 2, N_TOK])
                    v["kt"] = part("kt", [P, 1, N_TOK])
                    v["ck"] = part("ck", [P, KV_HEADS if kind in "AB" else HEADS // 2, N_PAST])
                    v["cv"] = part("cv", [P, (KV_HEADS if kind in "AB" else HEADS) * HD])
                    v["oT_hi"] = part("oT_hi", [P, KD, N_TOK], F32R)
                    v["oT_lo"] = part("oT_lo", [P, KD, N_TOK], F32R)
                    if kind in "AB":
                        v["rope"] = part("rope", [P, 2, nh * HD])
                        v["cos"] = part("cos", [P, 2, HD])
                        v["sin"] = part("sin", [P, 2, HD])
                        v["cg"] = part("cg", [P, 2, nh * HD])
                        v["sg"] = part("sg", [P, 2, nh * HD])
                    if kind == "A":
                        v["mask"] = part("mask", [P, 2, P])
                        v["sink"] = part("sink", [P, HEADS])
                        v["sink8"] = part("sink8", [P, HEADS])
                    if kind == "D":
                        v["bias"] = [part(f"bias{i}", [P, 2, 6, GRID_W]) for i in range(2)]
                        v["mask"] = part("mask", [P, GRID_W])
        act_hi, act_lo = tiles["F"]["act_hi"], tiles["F"]["act_lo"]
        sil, prod = sq, tmp
        acc, boot = tiles["F"]["acc"], tiles["F"]["boot"]
        acc_of_scale = w_raw[1][:, 0:2 * D].rearrange("p (c d) -> p c d", c=2)

        mixer_loads = {
            "A": ["g", "cos", "sin", "mask", "sink", "ck", "cv"],
            "B": ["g", "cos", "sin", "ck", "cv"],
            "C": ["g", "gd", "cos", "sin", "cache", "kr"],
            "D": ["g", "mask", "ck", "cv"],
        }
        n_loads, total = {}, 0
        for kind in "ABCD":
            total += 16 * len(mixer_loads[kind])
            n_loads[kind] = total

        w_dram = {"gu": a["ffn_gu"], "dn": a["ffn_dn"]}
        scale_of = {"A": HD ** -0.5, "B": HD ** -0.5, "C": C_QK ** -0.5, "D": HD ** -0.5}
        n_down = {"A": 0, "B": 0, "C": 2, "D": 0}

        def chunk_src(s, c):
            kind, c = stage_kind(s), c - n_down[stage_kind(s)]
            if c < 0:
                return a["c_dn0" if c == -2 else "c_dn1"], KD * C_DOWN_COLS[c + 2]
            if c < GROUPS[kind]:
                return a[kind.lower() + "_w"][c], C_UP_CHUNK if kind == "C" else QKV_CHUNK
            return a[kind.lower() + "_wo"][c - GROUPS[kind]], WO_CHUNK

        def width(s, c):
            if c == CB[s + 1] - CB[s]:
                return width(s + 1, 0) if s + 1 < N_STAGE else 0
            if stage_kind(s) == "F":
                return GU_CHUNK if c < GU_STEPS else DN_CHUNK
            return chunk_src(s, c)[1]

        def landed(n):
            return 8 * n + 16

        def scaled_to(part, k):
            return KD * (part - 1) + k + 1

        def added_to(part, k):
            return (KD - 1) * (part - 1) + k

        def summed_to(part, k):
            return KD * part + k + 1

        block = ctx.enter_context(nc.Block())

        @block.sync
        def _(sp):
            def load_w(n, par, dst_w, src):
                sp.wait_ge(w_split_lo.sem, n + par + 1)
                sp.dma_start(w_raw[par][:, 0:dst_w], src).then_inc(w_landed[par], 16)

            def load_gu(s, j, par):
                f = 2 * (s // 3) + (s % 3 == 2)
                load_w(CB[s] + j - par, par, GU_CHUNK,
                       w_dram["gu"][bass.ds(f * GU_STEPS + j, 1)].rearrange("o p c -> (o p) c"))

            def load_slab(part, k):
                sp.wait_ge(slab_summed, summed_to(part, k) - SLAB_SLOTS)
                sp.dma_start(slab[k % SLAB_SLOTS][:], a["mod_w"][bass.ds(KD * part + k, 1)].rearrange(
                    "o p c -> (o p) c")).then_inc(slab_landed[k % SLAB_SLOTS], 16)

            def load_part(s, i):
                for q in range(4):
                    load_gu(s, 4 * i + q + 2, q % 2)
                    for k in SLABS[q]:
                        load_slab(first_part(s) + i, k)

            sp.dma_start(cond[:], a["cond"]).then_inc(cond_in, 16)
            for i in range(3 * KD // BOOT_BATCH):
                if i >= BOOT_FLIGHT:
                    n = i - BOOT_FLIGHT
                    sp.wait_ge(boot_landed[n % BOOT_SLOTS], 16 * (n // BOOT_SLOTS + 1))
                if i >= BOOT_SLOTS:
                    sp.wait_ge(slab_summed, BOOT_BATCH * (i - BOOT_SLOTS + 1))
                sp.dma_start(boot[i % BOOT_SLOTS][:], a["mod_w"][i * BOOT_BATCH:(i + 1) * BOOT_BATCH].rearrange(
                    "t p c -> p t c")).then_inc(boot_landed[i % BOOT_SLOTS], 16)
                if i == BOOT_SLOTS - 2:
                    sp.dma_start(x[:], a["x"]).then_inc(x_in, 16)
                    for dst, name in ((ident, "ident"), (mod_b, "mod_b"), (gains, "gains")):
                        sp.dma_start(dst[:], a[name]).then_inc(consts_in, 16)
            for s in range(N_STAGE):
                f = 2 * (s // 3) + (s % 3 == 2)
                if stage_kind(s) == "F":
                    for par in range(2):
                        if s == 0 and par == 1:
                            sp.wait_ge(part_turned, 2)
                        load_gu(s, par, par)
                    load_part(s, 0)
                    if n_parts(s) > 1:
                        with sp.Fori(1, n_parts(s)) as i:
                            load_part(s, i)
                    if 2 * n_parts(s) + 1 < GU_STEPS // 2:
                        with sp.Fori(2 * n_parts(s) + 1, GU_STEPS // 2) as pair:
                            i = 2 * pair
                            for par in range(2):
                                load_gu(s, i + par, par)
                    sp.wait_ge(slab_summed, summed_to(first_part(s) + n_parts(s) - 1, KD - 1))
                    with sp.Fori(0, DN_STEPS // 2) as pair:
                        i = 2 * pair
                        for par in range(2):
                            load_w(CB[s] + GU_STEPS + i, par, DN_CHUNK,
                                   w_dram["dn"][bass.ds(f * DN_STEPS + i + par, 1)].rearrange("o p c -> (o p) c"))
                else:
                    for c in range(CB[s + 1] - CB[s]):
                        src, n = chunk_src(s, c)
                        load_w(CB[s] + c - c % 2, c % 2, n, src)
            sp.wait_ge(x_updated.sem, x_updated.after(N_STAGE - 1, KD - 1))
            sp.dma_start(out["y"], x[:]).then_inc(out_done, 16)
            sp.wait_ge(out_done, 16)

        @block.gpsimd
        def _(pool):
            pool.memset(ones[:], 1.0).then_inc(pool_step, 1)
            pool.memset(neghalf[:], -0.5).then_inc(pool_step, 1)
            pool.wait_ge(pool_step, 2)
            chain = Chain(pool, pool_step)
            chain.base = 2

            def power(dst, src, ready, key, done):
                pool.wait_ge(ready.sem, ready.after(key))
                n = src.shape[1]
                pool.tensor_tensor(dst, src, neghalf[:, 0:n], ALU.pow).then_inc(done.sem, 1)

            def scale_heads(s, g):
                kind = stage_kind(s)
                v = tiles[kind]
                pool.wait_ge(hrs_ready.sem, hrs_ready.after((s, g)))
                if kind != "C":
                    nh = HPG[kind] + KVPG[kind]
                    raw = v["raw"][g % 3][:, :, 0:nh * HD].rearrange("p t (h d) -> p t h d", h=nh)
                    r = v["hrs"][:, 0:TT * nh].rearrange("p (t h) -> p t h", h=nh).unsqueeze(3)
                    pool.tensor_tensor(v["nrm"].rearrange("p t (h d) -> p t h d", h=nh), raw,
                                       r.to_broadcast([P, TT, nh, HD]), ALU.mult).then_inc(head_scaled.sem, 1)
                    return
                regions = ((slice(0, TT), slice(0, 2), 6, 0), (slice(0, 4), slice(2, 4), 8, 6))
                for i, (t, h, n, at) in enumerate(regions):
                    r = v["hrs"][:, at:at + n].rearrange("p (t h) -> p t h", h=2).unsqueeze(3)
                    z = v["cat"][g % 2][:, t, h, :]
                    chain.link(pool.tensor_tensor(z, z, r.to_broadcast([P, n // 2, 2, C_QK]), ALU.mult))
                    gain = v["g"][:, i, :].unsqueeze(1).unsqueeze(1).to_broadcast([P, n // 2, 2, C_QK])
                    ins = pool.tensor_tensor(z, z, gain, ALU.mult)
                    if i == 0:
                        chain.link(ins)
                ins.then_inc(head_scaled.sem, 1)

            def add_slab(part, k, sums):
                pool.wait_ge(slab_scaled, scaled_to(part, k))
                if k > 1:
                    pool.wait_ge(slab_added, added_to(part, k - 1))
                pool.tensor_tensor(sums[:, 0, :], sums[:, 0, :], scaled[k % 2][:], ALU.add).then_inc(slab_added, 1)

            for part, sums in ((1, acc_of_scale), (2, acc)):
                for k in range(1, KD):
                    add_slab(part, k, sums)
            for s in range(N_STAGE):
                kind = stage_kind(s)
                power(rstd[:, 0:TT], msq[:, 0:TT], ms_ready, s, rstd_ready)
                if kind == "F":
                    for k in range(1, KD):
                        add_slab(first_part(s), k, acc)
                    if n_parts(s) > 1:
                        with pool.Fori(1, n_parts(s)) as i:
                            for k in range(1, KD):
                                add_slab(first_part(s) + i, k, acc)
                    continue
                v = tiles[kind]
                pool.wait_ge(w_used.sem, w_used.at[s])
                for name in mixer_loads[kind]:
                    dst = v[name][:, 3, :] if name == "kr" else v[name][:]
                    pool.dma_start(dst, a[f"{kind.lower()}_{name}"]).then_inc(mixer_in, 16)

                def load_bias(g):
                    if g >= 2:
                        pool.wait_ge(qkt_made.sem, qkt_made.after((s, g - 1)))
                    for rl in range(2):
                        for h in range(2):
                            src = a["d_rpb"]
                            at = ((2 * g + h) * RPB_R + 5 - rl) * RPB_W
                            pool.dma_start(v["bias"][g % 2][GRID_W * rl:GRID_W * (rl + 1), h],
                                           bass.AP(tensor=src.tensor, offset=src.offset + at,
                                                   ap=[[1, GRID_W], [RPB_W, 6], [1, GRID_W]])
                                           ).then_inc(bias_in[g % 2], 16)

                if kind == "D":
                    load_bias(0)
                    load_bias(1)
                def rotary_key(g):
                    for h in (2, 3):
                        ins = pool.tensor_copy(v["cat"][g % 2][:, :, h, C_NOPE:C_QK], v["kr"][:])
                    ins.then_inc(kr_ready.sem, 1)

                if kind == "C":
                    power(v["crs"].rearrange("p a b -> p (a b)"), v["cms"].rearrange("p a b -> p (a b)"),
                          c_norm_ready, "ms", c_rstd_ready)
                    pool.wait_ge(c_norm_ready.sem, c_norm_ready.after("cq"))
                    pool.wait_ge(mixer_in, n_loads[kind])
                    rotary_key(0)
                    rotary_key(1)
                    for name, src in (("new_c_kv", v["cdn"][:, 0, C_Q_RANK:C_Q_RANK + C_KV_RANK]),
                                      ("new_c_krope", v["cdn"][:, 0, C_Q_RANK + C_KV_RANK:C_DOWN])):
                        pool.dma_start(out[name], src).then_inc(kv_out, 16)
                for g in range(GROUPS[kind]):
                    nh = {"A": 15, "B": 15, "C": 14, "D": 12}[kind]
                    power(v["hrs"][:, 0:nh], v["hms"][:, 0:nh], hms_ready, (s, g), hrs_ready)
                    scale_heads(s, g)
                    if kind == "C" and g + 2 < GROUPS[kind]:
                        pool.wait_ge(qkt_made.sem, qkt_made.after((s, g), 3))
                        rotary_key(g + 2)
                    if kind == "D" and 1 <= g and g + 1 < GROUPS[kind]:
                        load_bias(g + 1)
                    if kind != "C":
                        kw = KVPG[kind] * HD
                        pool.wait_ge(qn_ready.sem, qn_ready.after((s, g)))
                        pool.dma_start(out[f"new_{kind.lower()}_k"][:, g * kw:(g + 1) * kw],
                                       v["qn"][:, 0, HPG[kind] * HD:HPG[kind] * HD + kw]).then_inc(kv_out, 16)
                        pool.dma_start(out[f"new_{kind.lower()}_v"][:, g * kw:(g + 1) * kw],
                                       v["raw"][g % 3][:, 0, QKV_W - kw:QKV_W]).then_inc(kv_out, 16)
            pool.wait_ge(kv_out, kv_sent[N_STAGE - 1])

        @block.tensor
        def _(pe):
            chain = Chain(pe, pe_step)
            pe.sem_inc(w_used.sem, 2)

            def turn_part(part, sums):
                pe.wait_ge(slab_summed, summed_to(part, KD - 1))
                if not isinstance(part, int) or part > 0:
                    pe.wait_ge(slab_added, added_to(part, KD - 1))
                    pe.wait_ge(part_read, part)
                for i in range(2 * KD):
                    mm = pe.transpose(ps[:, B_PART + i // 4, i % 4 * P:(i % 4 + 1) * P],
                                      sums.rearrange("p c d -> p (c d)")[:, i * P:(i + 1) * P], ident[:])
                mm.then_inc(part_turned, 1)

            def norm(s):
                pe.wait_ge(ssq_ready.sem, ssq_ready.after(s - 1, KD - 1))
                for t in range(TT):
                    mm = pe.matmul(ps[:, B_NORM, t:t + 1], ssq[:, t * P:(t + 1) * P], ones[:, 0:1],
                                   start=True, stop=True)
                mm.then_inc(stats_made.sem, 1)
                pe.wait_ge(diag_ready.sem, diag_ready.after(s))
                pe.matmul(ps[:, B_NORM, 0:N_TOK], ones[:], diag.rearrange("p t c -> p (t c)"),
                          start=True, stop=True).then_inc(rbc_made.sem, 1)

            def gu_first(s):
                pe.wait_ge(w_split_lo.sem, w_split_lo.after(s, 0))
                w = [q[0][:, 0:GU_CHUNK].rearrange("p (k u c) -> p k u c", k=KD, u=2) for q in (w_hi, w_lo)]
                for k in range(KD):
                    pe.wait_ge(h_ready.sem, h_ready.after(s, k))
                    for u in range(2):
                        for i, (lh, rh) in enumerate(((w[0], h_hi), (w[0], h_lo), (w[1], h_hi))):
                            mm = pe.matmul(ps[:, u, 0:N_TOK], lh[:, k, u, :], rh[:, k, :],
                                           start=(k == 0 and i == 0), stop=(k == KD - 1 and i == 2))
                mm.then_inc(w_used.sem, 1)

            def gu_step(s, j, par):
                pe.wait_ge(w_split_hi.sem, w_split_hi.after(s, j))
                pe.wait_ge(prod_ready.sem, prod_ready.at[s] + j - 1)
                w = [q[par][:, 0:GU_CHUNK].rearrange("p (k u c) -> p k u c", k=KD, u=2) for q in (w_hi, w_lo)]
                for u in range(2):
                    for k in range(KD):
                        for h in (h_hi, h_lo):
                            pe.matmul(ps[:, 2 * par + u, 0:N_TOK], w[0][:, k, u, :], h[:, k, :],
                                      start=(k == 0 and h is h_hi), stop=False)
                pe.wait_ge(w_split_lo.sem, w_split_lo.after(s, j))
                for u in range(2):
                    for k in range(KD):
                        mm = pe.matmul(ps[:, 2 * par + u, 0:N_TOK], w[1][:, k, u, :], h_hi[:, k, :],
                                       start=False, stop=(k == KD - 1))
                mm.then_inc(w_used.sem, 1)

            def dn_step(s, m, par, first=False):
                c = GU_STEPS + m
                pe.wait_ge(w_split_hi.sem, w_split_hi.after(s, c))
                pe.wait_ge(x_updated.sem, x_updated.at[s] + m - 1)
                if first:
                    pe.wait_ge(prod_ready.sem, prod_ready.after(s, GU_STEPS - 2))
                    pe.wait_ge(act_ready.sem, act_ready.after(s, KF - 3))
                for k in range(KF):
                    if first and k >= KF - 2:
                        pe.wait_ge(act_ready.sem, act_ready.after(s, k))
                    for y in (act_hi, act_lo):
                        pe.matmul(ps[:, par, 0:N_TOK], w_hi[par][:, k * P:(k + 1) * P],
                                  y[:, k * N_TOK:(k + 1) * N_TOK], start=(k == 0 and y is act_hi), stop=False)
                pe.wait_ge(w_split_lo.sem, w_split_lo.after(s, c))
                for k in range(KF):
                    mm = pe.matmul(ps[:, par, 0:N_TOK], w_lo[par][:, k * P:(k + 1) * P],
                                   act_hi[:, k * N_TOK:(k + 1) * N_TOK], start=False, stop=(k == KF - 1))
                mm.then_inc(w_used.sem, 1)

            def split_product(bank, cols, left, right, n, rows=P):
                for k in range(n):
                    for i, (lh, rh) in enumerate(((0, 0), (0, 1), (1, 0))):
                        mm = pe.matmul(ps[0:rows, bank, cols[0]:cols[1]], left(lh, k), right(rh, k),
                                       start=(k == 0 and i == 0), stop=(k == n - 1 and i == 2))
                return mm

            def project(s, g, t, k):
                kind = stage_kind(s)
                v = tiles[kind]
                par = (n_down[kind] + g) % 2
                rh = (w_hi[par], w_lo[par])
                if kind != "C":
                    parts = [((h_hi, h_lo), 0, QKV_W, 0, KD)]
                else:
                    parts = [((v["ckT_hi"], v["ckT_lo"]), KQ * C_UQ_W, C_UKV_W, C_UQ_W, KC)]
                    if t < TT:
                        parts = [((v["cqT_hi"], v["cqT_lo"]), 0, C_UQ_W, 0, KQ)] + parts
                for lh, at, w, col, n in parts:
                    for k1 in range(n) if k is None else (k,):
                        for i, (x1, x2) in enumerate(((0, 0), (0, 1), (1, 0))):
                            mm = pe.matmul(ps[:, proj_bank(g, t), col:col + w], lh[x1][:, k1, t * P:(t + 1) * P],
                                           rh[x2][:, at + k1 * w:at + (k1 + 1) * w],
                                           start=(k1 == 0 and i == 0), stop=(k1 == n - 1 and i == 2))
                if k is None or k == KD - 1:
                    mm.then_inc(*((w_used.sem, 1) if t == proj_tiles(kind) - 1 else (proj_made.sem, 1)))

            def projection(s, g, t):
                kind = stage_kind(s)
                c = n_down[kind] + g
                if t == 0:
                    pe.wait_ge(w_split_hi.sem, w_split_hi.after(s, c))
                    pe.wait_ge(w_split_lo.sem, w_split_lo.after(s, c))
                if t >= 2:
                    pe.wait_ge(raw_ready.sem, raw_ready.after((s, g), t - 2))
                else:
                    pe.wait_ge(raw_ready.sem, raw_ready.after((s, g - 1), proj_tiles(kind) - 1))
                project(s, g, t, None)

            def first_projection(s):
                kind = stage_kind(s)
                c = n_down[kind]
                pe.wait_ge(w_split_hi.sem, w_split_hi.after(s, c))
                pe.wait_ge(w_split_lo.sem, w_split_lo.after(s, c))
                for k in (None,) if kind == "C" else range(KD):
                    if k is not None:
                        pe.wait_ge(h_ready.sem, h_ready.after(s, k))
                    for t in range(proj_tiles(kind)):
                        project(s, 0, t, k)

            def turn_qk(s, g, first, last):
                kind = stage_kind(s)
                v = tiles[kind]
                pe.wait_ge(qn_ready.sem, qn_ready.after((s, g)))
                if g + 1 < GROUPS[kind]:
                    pe.wait_ge(raw_ready.sem, raw_ready.after((s, g + 1), proj_tiles(kind) - 1))
                for i, (what, n, w) in list(enumerate(qkt_types(kind)))[first:last]:
                    bank = QKT_BANKS[i]
                    if bank in B_S and g >= 1:
                        pe.wait_ge(exp_ready.sem, exp_ready.after((s, g - 1, len(units(kind)) - 1)))
                    if kind == "C":
                        col = n + (2 if what == "k" else 0)
                        for t in range(4 if what == "k" else TT):
                            mm = pe.transpose(ps[0:w, bank, t * P:(t + 1) * P], v["cat"][g % 2][:, t, col, :], ident[:])
                    else:
                        at = n * P if what == "q" else HPG[kind] * HD
                        for t in range(TT):
                            mm = pe.transpose(ps[:, bank, t * P:(t + 1) * P], v["qn"][:, t, at:at + P], ident[:])
                    mm.then_inc(qkt_made.sem, 1)

            def scores(s, g, u, uu):
                kind = stage_kind(s)
                v = tiles[kind]
                what, h, t = units(kind)[u]
                bank = B_S[uu % 2]
                if u == 0:
                    pe.wait_ge(qkt_ready.sem, qkt_ready.after((s, g), len(qkt_types(kind)) - 1))
                if uu - 2 >= first_unit[s]:
                    pe.wait_ge(exp_ready.sem, exp_ready.at[(s, g, u)] - 1)
                heads = (h,)
                if what == "ctx":
                    heads = sorted(range(HPG[kind]), key=lambda h: h % 2)
                for h in heads:
                    if kind == "C":
                        q = v["qt"][0:C_QK, h, t * P:(t + 1) * P]
                        k = v["kt"][0:C_QK, h, :]
                    else:
                        half = slice(HD * (h % 2), HD * (h % 2) + HD)
                        q = v["qt"][half, h // 2, t * P:(t + 1) * P]
                        k = v["kt"][half, 0, :]
                    if what == "ctx":
                        mm = pe.matmul(ps[:, bank, h * P:(h + 1) * P], q, k[:, 0:P], start=True, stop=True)
                        if kind != "C" and h == HPG[kind] - 2:
                            chain.link(mm)
                    elif kind == "C":
                        mm = pe.matmul(ps[:, bank, 0:N_LAT + N_PAST], q, k[:, P:P + N_LAT + N_PAST],
                                       start=True, stop=True)
                    else:
                        cache = v["ck"][half, g, :]
                        pe.matmul(ps[:, bank, 0:N_LAT], q, k[:, P:P + N_LAT], start=True, stop=True)
                        mm = pe.matmul(ps[:, bank, N_LAT:N_LAT + N_PAST], q, cache, start=True, stop=True)
                mm.then_inc(s_made.sem, 1)

            def turn_p(s, g, u, uu):
                kind = stage_kind(s)
                what, _, _ = units(kind)[u]
                pe.wait_ge(p_scaled.sem, p_scaled.after((s, g, u)))
                if uu - 2 >= first_unit[s]:
                    pe.wait_ge(pt_ready.sem, pt_ready.at[(s, g, u)] - 1)
                for n in range(HPG[kind] if what == "ctx" else 3):
                    mm = pe.transpose(ps[:, B_PT[uu % 2], n * P:(n + 1) * P],
                                      tiles[kind]["p"][uu % 3][:, n * P:(n + 1) * P], ident[:])
                mm.then_inc(pt_made.sem, 1)

            def values(s, g, u, uu):
                kind = stage_kind(s)
                v = tiles[kind]
                what, h, t = units(kind)[u]
                pt = v["pt"][uu % 2]
                pe.wait_ge(pt_ready.sem, pt_ready.after((s, g, u)))
                ahead = 1 if HPG[kind] > 2 else 2
                if u >= 1:
                    pe.wait_ge(o_made.sem, o_made.at[(s, g, u)])
                elif g >= ahead:
                    pe.wait_ge(ot_ready.sem, ot_ready.after((s, g - ahead)))

                def out(h, t):
                    rows = slice(HD * (h % 2), HD * (h % 2) + HD)
                    return ps[rows, out_bank(kind, g, h // 2), t * P:(t + 1) * P]

                def val(t, h):
                    if kind == "C":
                        return v["v"][g % 3][:, t, h * HD:(h + 1) * HD]
                    kvh = h * KVPG[kind] // HPG[kind]
                    at = QKV_W - KVPG[kind] * HD + kvh * HD
                    if t == 3:
                        at = (g * KVPG[kind] + kvh) * HD
                        return v["cv"][:, at:at + HD]
                    return v["raw"][g % 3][:, t, at:at + HD]

                if what == "ctx":
                    for h in sorted(range(HPG[kind]), key=lambda h: h % 2):
                        mm = pe.matmul(out(h, 0), val(0, h), pt[:, h * P:(h + 1) * P], start=True, stop=True)
                        if h == HPG[kind] - 2:
                            chain.link(mm)
                else:
                    for n in range(3):
                        mm = pe.matmul(out(h, t), val(n + 1, h), pt[:, n * P:(n + 1) * P],
                                       start=(n == 0), stop=(n == 2))
                mm.then_inc(o_made.sem, 1)

            def compress(s):
                v = tiles["C"]
                for c in range(2):
                    w = C_DOWN_COLS[c]
                    pe.wait_ge(w_split_hi.sem, w_split_hi.after(s, c))
                    pe.wait_ge(w_split_lo.sem, w_split_lo.after(s, c))
                    if c == 0:
                        for k in range(KD):
                            pe.wait_ge(h_ready.sem, h_ready.after(s, k))
                            for t in range(TT):
                                for i, (lh, rh) in enumerate(((h_hi, w_hi), (h_hi, w_lo), (h_lo, w_hi))):
                                    mm = pe.matmul(ps[:, C_BANKS[0][t], 0:w], lh[:, k, t * P:(t + 1) * P],
                                                   rh[0][:, k * w:(k + 1) * w],
                                                   start=(k == 0 and i == 0), stop=(k == KD - 1 and i == 2))
                        mm.then_inc(w_used.sem, 1)
                        continue
                    for t in range(TT):
                        mm = split_product(
                            C_BANKS[c][t], (0, w),
                            lambda i, k: (h_hi, h_lo)[i][:, k, t * P:(t + 1) * P],
                            lambda i, k: (w_hi, w_lo)[i][c][:, k * w:(k + 1) * w], KD)
                    mm.then_inc(w_used.sem, 1)
                pe.wait_ge(c_norm_ready.sem, c_norm_ready.after("cq"))
                for n in range(KQ + KC):
                    for t in range(TT):
                        mm = pe.transpose(ps[:, CT_BANKS[n], t * P:(t + 1) * P],
                                          v["cdn"][:, t, n * P:(n + 1) * P], ident[:])
                    mm.then_inc(c_t_made, 1)
                pe.wait_ge(c_t_ready, KQ + KC + 1)

            pe.wait_ge(pool_step, 2)
            pe.wait_ge(consts_in, 16 * 3)
            for part in range(3):
                turn_part(part, acc_of_scale if part == 1 else acc)
            uu = 0
            for s in range(N_STAGE):
                norm(s)
                kind = stage_kind(s)
                if kind == "F":
                    gu_first(s)
                    for j in range(1, 4):
                        gu_step(s, j, j % 2)
                    turn_part(first_part(s), acc)
                    if n_parts(s) > 1:
                        with pe.Fori(1, n_parts(s)) as i:
                            for q in range(4):
                                gu_step(s, 4 * i + q, q % 2)
                            turn_part(first_part(s) + i, acc)
                    with pe.Fori(2 * n_parts(s), GU_STEPS // 2) as pair:
                        i = 2 * pair
                        for par in range(2):
                            gu_step(s, i + par, par)
                    dn_step(s, 0, 0, True)
                    dn_step(s, 1, 1)
                    with pe.Fori(1, DN_STEPS // 2) as pair:
                        i = 2 * pair
                        for par in range(2):
                            dn_step(s, i + par, par)
                    continue
                n_g, n_u = GROUPS[kind], len(units(kind))
                if kind == "C":
                    compress(s)
                first_projection(s)
                for t in range(proj_tiles(kind)):
                    projection(s, 1, t)
                turn_qk(s, 0, 0, 4)
                pe.wait_ge(mixer_in, n_loads[kind])
                for g in range(n_g):
                    more = g + 2 < n_g
                    for u in range(n_u + 3):
                        if u == n_u + 1 and g + 1 < n_g:
                            turn_qk(s, g + 1, 2, 4)
                        if u < n_u:
                            scores(s, g, u, uu + u)
                        if u < 2 and more:
                            projection(s, g + 2, u)
                        if 2 <= u < n_u + 2:
                            turn_p(s, g, u - 2, uu + u - 2)
                        if u == 2 and more:
                            for t in range(2, proj_tiles(kind)):
                                projection(s, g + 2, t)
                        if u >= 3:
                            values(s, g, u - 3, uu + u - 3)
                        if u == n_u and g + 1 < n_g:
                            turn_qk(s, g + 1, 0, 2)
                    uu += n_u
                pe.wait_ge(ot_ready.sem, ot_ready.after((s, n_g - 1)))
                v = tiles[kind]
                for c in range(WO_STEPS):
                    n = n_down[kind] + n_g + c
                    par = n % 2
                    pe.wait_ge(w_split_hi.sem, w_split_hi.after(s, n))
                    pe.wait_ge(w_split_lo.sem, w_split_lo.after(s, n))
                    for b in range(2):
                        pe.wait_ge(x_updated.sem, x_updated.at[s] + 2 * c + b - 1)
                        at = lambda k: slice(k * 2 * P + b * P, k * 2 * P + (b + 1) * P)
                        mm = split_product(b, (0, N_TOK),
                                           lambda i, k: (w_hi, w_lo)[i][par][:, at(k)],
                                           lambda i, k: (v["oT_hi"], v["oT_lo"])[i][:, k, :], KD)
                        mm.then_inc(wo_half.sem if b == 0 else w_used.sem, 1)

        @block.scalar
        def _(act):
            chain = Chain(act, act_step)

            def split_hi(n, par, w):
                act.wait_ge(w_landed[par], landed(n))
                act.wait_ge(w_used.sem, n + par + 1)
                act.activation(w_hi[par][:, 0:w], w_raw[par][:, 0:w], ACT.Copy).then_inc(w_split_hi.sem, 1)

            def modulated_hi(s, k):
                act.wait_ge(xr_ready.sem, xr_ready.after(s, k))
                shift = mod[:, 3 * KD * (s % 3) + k, :]
                act.activation(h_hi[:, k, 0:P], tmp[k % 2][:, 0:P], ACT.Identity, bias=shift[:, 0:1])
                act.activation(h_hi[:, k, P:N_TOK], tmp[k % 2][:, P:N_TOK], ACT.Identity,
                               bias=shift[:, 1:2]).then_inc(h_hi_ready.sem, 1)

            def scale_slab(part, k, w, sums):
                if k == 0 and isinstance(part, int) and part < 3:
                    if part == 2:
                        act.wait_ge(part_turned, 1)
                        act.wait_ge(slab_added, added_to(1, KD - 1))
                elif k == 0:
                    act.wait_ge(part_turned, part)
                elif k > 2:
                    act.wait_ge(slab_added, added_to(part, k - 2))
                act.activation(sums[:, 0, :] if k == 0 else scaled[k % 2][:], w, ACT.Copy,
                               scale=cond[:, k, 0:1]).then_inc(slab_scaled, 1)

            def square(s, m, par):
                act.wait_ge(x_updated.sem, x_updated.after(s, m))
                act.activation(sq[par][:], x[:, m, :] if isinstance(m, int) else
                               x[:, bass.ds(m, 1), :].rearrange("p o t -> p (o t)"),
                               ACT.Square).then_inc(sq_ready.sem, 1)

            def gu_step(s, j, par, w_next, part=None, slabs=()):
                def scale_next(ks):
                    for k in ks:
                        act.wait_ge(slab_landed[k % SLAB_SLOTS], 32 * (part - 3) + 16 * (k // SLAB_SLOTS + 1))
                        scale_slab(part, k, slab[k % SLAB_SLOTS], acc)

                split_hi(CB[s] + j + 1 - (1 - par), 1 - par, w_next)
                scale_next(slabs[0:2])
                act.wait_ge(w_used.sem, w_used.after(s, j))
                act.activation(sil[par][:], ps[:, 2 * par, 0:N_TOK], ACT.Silu).then_inc(silu_ready.sem, 1)
                act.wait_ge(prod_ready.sem, prod_ready.after(s, j))
                act.activation(act_hi[:, bass.ds(j * N_TOK, N_TOK)], prod[par][:],
                               ACT.Copy).then_inc(act_hi_ready.sem, 1)
                scale_next(slabs[2:])

            def dn_step(s, m, par, w_next):
                if w_next:
                    split_hi(CB[s] + GU_STEPS + m + 1 - (1 - par), 1 - par, w_next)
                square(s, m, par)

            def raw(s, g, t):
                kind = stage_kind(s)
                v = tiles[kind]
                last = t == proj_tiles(kind) - 1
                if last:
                    act.wait_ge(w_used.sem, w_used.after(s, n_down[kind] + g))
                else:
                    act.wait_ge(proj_made.sem, proj_made.after((s, g), t))
                if t == 0 and g >= 3 and kind != "C":
                    act.wait_ge(kv_out, kv_sent[s, g - 2])
                bank = ps[:, proj_bank(g, t), :]
                if kind != "C":
                    act.activation(v["raw"][g % 3][:, t, :], bank[:, 0:QKV_W], ACT.Copy).then_inc(raw_ready.sem, 1)
                    return
                if t == 0:
                    act.wait_ge(kr_ready.sem, kr_ready.after((s, g)))
                kv = bank[:, C_UQ_W:C_UQ_W + C_UKV_W].rearrange("p (h x d) -> p h x d", h=2, x=2)
                if t < TT:
                    act.activation(v["cat"][g % 2][:, t, 0:2, :].rearrange("p h d -> p (h d)"), bank[:, 0:C_UQ_W], ACT.Copy)
                act.activation(v["v"][g % 3][:, t, :].rearrange("p (h d) -> p h d", h=2), kv[:, :, 1, :], ACT.Copy)
                act.activation(v["cat"][g % 2][:, t, 2:4, 0:C_NOPE], kv[:, :, 0, :], ACT.Copy).then_inc(raw_ready.sem, 1)

            def squares_of(s, g):
                kind = stage_kind(s)
                v = tiles[kind]
                act.wait_ge(raw_ready.sem, raw_ready.after((s, g), proj_tiles(kind) - 1))
                if kind != "C":
                    nn = (HPG[kind] + KVPG[kind]) * HD
                    act.activation(v["nrm"][:], v["raw"][g % 3][:, :, 0:nn], ACT.Square).then_inc(rsq_ready.sem, 1)
                    return
                act.activation(v["sqc"][:, 0:TT, 0:2, :], v["cat"][g % 2][:, 0:TT, 0:2, :], ACT.Square)
                act.activation(v["sqc"][:, :, 2:4, :], v["cat"][g % 2][:, :, 2:4, :], ACT.Square
                               ).then_inc(rsq_ready.sem, 1)

            def qk_copies(s, g, first, last):
                kind = stage_kind(s)
                v = tiles[kind]
                for i, (what, n, w) in list(enumerate(qkt_types(kind)))[first:last]:
                    act.wait_ge(qkt_made.sem, qkt_made.after((s, g), i))
                    dst = v["kt" if what == "k" else "qt"][0:w, n if what == "q" or kind == "C" else 0, :]
                    act.activation(dst, ps[0:w, QKT_BANKS[i], 0:dst.shape[1]], ACT.Copy).then_inc(qkt_ready.sem, 1)

            def probabilities(s, g, u, uu):
                kind = stage_kind(s)
                v = tiles[kind]
                what, h, t = units(kind)[u]
                st, p = v["stat"], v["p"][uu % 3]
                act.wait_ge(max_ready.sem, max_ready.after((s, g, u)))
                if uu >= 3 and uu - 3 >= first_unit[s]:
                    act.wait_ge(pt_made.sem, pt_made.at[(s, g, u)] - 2)
                n = HPG[kind] if what == "ctx" else 1
                w = P if what == "ctx" else N_LAT + N_PAST
                for i in range(n):
                    ins = act.activation(p[:, i * w:(i + 1) * w], ps[:, B_S[uu % 2], i * w:(i + 1) * w], ACT.Exp,
                                         bias=st[:, uu % 3, 1, i:i + 1], scale=scale_of[kind],
                                         accum_out=st[:, uu % 3, 2, i:i + 1])
                if kind == "A":
                    ins = act.activation(st[:, uu % 3, 3, 0:n], st[:, uu % 3, 3, 0:n], ACT.Exp)
                ins.then_inc(exp_ready.sem, 1)

            def p_copy(s, g, u, uu):
                kind = stage_kind(s)
                what, _, _ = units(kind)[u]
                w = P * (HPG[kind] if what == "ctx" else 3)
                act.wait_ge(pt_made.sem, pt_made.after((s, g, u)))
                if uu - 2 >= first_unit[s]:
                    act.wait_ge(o_made.sem, o_made.at[(s, g, u)] - 1)
                act.activation(tiles[kind]["pt"][uu % 2][:, 0:w], ps[:, B_PT[uu % 2], 0:w],
                               ACT.Copy).then_inc(pt_ready.sem, 1)

            def o_hi(s, g):
                kind = stage_kind(s)
                v = tiles[kind]
                act.wait_ge(o_made.sem, o_made.after((s, g, len(units(kind)) - 1)))
                for n in range(HPG[kind] // 2):
                    ins = act.activation(v["oT_hi"][:, g * HPG[kind] // 2 + n, :], ps[:, out_bank(kind, g, n), 0:N_TOK], ACT.Copy)
                ins.then_inc(ot_hi_ready.sem, 1)

            def compress(s):
                v = tiles["C"]
                for c in range(2):
                    split_hi(CB[s] + 2 * c, 1 - c, width(s, c + 1))
                    act.wait_ge(w_used.sem, w_used.after(s, c))
                    w, at = C_DOWN_COLS[c], C_Q_RANK * c
                    for t in range(TT):
                        chain.link(act.activation(v["cdn"][:, t, at:at + w], ps[:, C_BANKS[c][t], 0:w], ACT.Copy))
                    for t in range(TT):
                        w = (C_Q_RANK, C_KV_RANK)[c]
                        chain.link(act.activation(v["junk"][:, 0:w], v["cdn"][:, t, at:at + w], ACT.Square,
                                                  accum_out=v["cms"][:, c, t:t + 1]))
                act.sem_inc(c_raw_ready, 1)
                for n in range(KQ + KC):
                    act.wait_ge(c_t_made, n + 1)
                    dst = v["cqT_hi"][:, n, :] if n < KQ else v["ckT_hi"][:, n - KQ, 0:N_TOK]
                    act.activation(dst, ps[:, CT_BANKS[n], 0:N_TOK], ACT.Copy).then_inc(c_hi_ready, 1)
                act.wait_ge(mixer_in, n_loads["C"])
                act.activation(v["ckT_hi"][:, :, N_TOK:N_TOK + N_PAST], v["cache"][:], ACT.Copy).then_inc(c_hi_ready, 1)

            def squares():
                for m in range(KD):
                    if m >= 2:
                        act.wait_ge(ssq_ready.sem, ssq_ready.after(-1, m - 2))
                    act.activation(sq[m % 2][:], x[:, m, :], ACT.Square).then_inc(sq_ready.sem, 1)

            act.wait_ge(cond_in, 16)
            chain.link(act.activation(cond[:], cond[:], ACT.Silu))
            for part, sums in ((1, acc_of_scale), (2, acc)):
                for k in range(KD):
                    n = part * KD + k
                    batch = n // BOOT_BATCH
                    act.wait_ge(boot_landed[batch % BOOT_SLOTS], 16 * (batch // BOOT_SLOTS + 1))
                    scale_slab(part, k, boot[batch % BOOT_SLOTS][:, n % BOOT_BATCH, :], sums)
            act.wait_ge(x_in, 16)
            squares()
            split_hi(0, 0, GU_CHUNK)
            uu = 0
            for s in range(N_STAGE):
                for k in range(KD):
                    modulated_hi(s, k)
                kind = stage_kind(s)
                if kind == "F":
                    if kv_sent[s]:
                        act.wait_ge(kv_out, kv_sent[s])
                    for q in range(4):
                        gu_step(s, q, q % 2, GU_CHUNK, first_part(s), SLABS[q])
                    if n_parts(s) > 1:
                        with act.Fori(1, n_parts(s)) as i:
                            for q in range(4):
                                gu_step(s, 4 * i + q, q % 2, GU_CHUNK, first_part(s) + i, SLABS[q])
                    if 2 * n_parts(s) < (GU_STEPS - 2) // 2:
                        with act.Fori(2 * n_parts(s), (GU_STEPS - 2) // 2) as pair:
                            i = 2 * pair
                            for par in range(2):
                                gu_step(s, i + par, par, GU_CHUNK)
                    gu_step(s, GU_STEPS - 2, 0, GU_CHUNK)
                    act.wait_ge(slab_added, added_to(first_part(s) + n_parts(s) - 1, KD - 1))
                    gu_step(s, GU_STEPS - 1, 1, DN_CHUNK)
                    with act.Fori(0, (DN_STEPS - 2) // 2) as pair:
                        i = 2 * pair
                        for par in range(2):
                            dn_step(s, i + par, par, DN_CHUNK)
                    dn_step(s, DN_STEPS - 2, 0, DN_CHUNK)
                    dn_step(s, DN_STEPS - 1, 1, width(s, GU_STEPS + DN_STEPS))
                    continue
                n_g, n_u, nd = GROUPS[kind], len(units(kind)), n_down[kind]

                def split_chunk(c):
                    if width(s, c):
                        split_hi(CB[s] + c - c % 2, c % 2, width(s, c))

                if kind == "C":
                    compress(s)
                split_chunk(nd + 1)
                for t in range(proj_tiles(kind)):
                    raw(s, 0, t)
                squares_of(s, 0)
                split_chunk(nd + 2)
                for t in range(proj_tiles(kind)):
                    raw(s, 1, t)
                qk_copies(s, 0, 0, 4)
                for g in range(n_g):
                    more = g + 2 < n_g
                    for u in range(n_u + 2):
                        if u == n_u + 1 and g + 1 < n_g:
                            qk_copies(s, g + 1, 2, 4)
                        if u == 0 and g + 1 < n_g:
                            squares_of(s, g + 1)
                        if u < n_u:
                            probabilities(s, g, u, uu + u)
                        if u == 1 and g >= 1:
                            o_hi(s, g - 1)
                        if u < 2 and more:
                            raw(s, g + 2, u)
                        if u == 1 and more:
                            split_chunk(nd + g + 3)
                        if u >= 2:
                            p_copy(s, g, u - 2, uu + u - 2)
                        if u == n_u and g + 1 < n_g:
                            qk_copies(s, g + 1, 0, 2)
                        if u == 2 and more:
                            for t in range(2, proj_tiles(kind)):
                                raw(s, g + 2, t)
                    uu += n_u
                o_hi(s, n_g - 1)
                for c in range(WO_STEPS):
                    split_chunk(nd + n_g + c + 1)
                    for b in range(2):
                        square(s, 2 * c + b, b)

        @block.vector
        def _(dve):
            chain = Chain(dve, dve_step)
            for c in (w_split_lo, prod_ready, act_ready, x_updated):
                dve.sem_inc(c.sem, 2)
            dve.sem_inc(ssq_ready.sem, 1)

            def split_lo(n, par, w):
                dve.wait_ge(w_split_hi.sem, n + par + 1)
                dve.tensor_tensor(w_lo[par][:, 0:w], w_raw[par][:, 0:w], w_hi[par][:, 0:w],
                                  ALU.subtract).then_inc(w_split_lo.sem, 1)

            def modulation(part, n):
                m = mod[:, part % N_PART * KD:(part % N_PART + n) * KD, :]
                chain.link(dve.tensor_tensor(m, m, mod_b[:, part * KD:(part + n) * KD].unsqueeze(2).to_broadcast(
                    [P, n * KD, 2]), ALU.add))
                for i in range(n):
                    q = (part + i) // 3
                    z = m[:, i * KD:(i + 1) * KD, :]
                    if (part + i) % 3 == 1:
                        chain.link(dve.scalar_tensor_tensor(out=z, in0=z, scalar=1.0,
                                                            in1=gains[:, q, :].unsqueeze(2).to_broadcast([P, KD, 2]),
                                                            op0=ALU.add, op1=ALU.mult))
                    if (part + i) % 3 == 2 and stage_kind(q) == "F":
                        chain.link(dve.tensor_scalar(z, z, FFN_RES, None, ALU.mult))

            def sum_slab(part, k, w, sums, kinds=(1,)):
                if k > 0:
                    dve.wait_ge(slab_summed, summed_to(part, k - 1))
                elif isinstance(part, int) and part < 3:
                    if part == 2:
                        dve.wait_ge(part_turned, 1)
                else:
                    dve.wait_ge(part_turned, part)
                for c in kinds:
                    if k == 0:
                        ins = dve.tensor_scalar(sums[:, c, :], w, cond[:, k, c:c + 1], None, ALU.mult)
                    else:
                        ins = dve.scalar_tensor_tensor(out=sums[:, c, :], in0=w, scalar=cond[:, k, c:c + 1],
                                                       in1=sums[:, c, :], op0=ALU.mult, op1=ALU.add)
                ins.then_inc(slab_summed, 1)

            def sum_partitions(part, at):
                dve.wait_ge(part_turned, part + 1)
                dve.tensor_reduce(mod[:, bass.ds(at * KD, KD), :].rearrange("p m c -> p c m"),
                                  ps[:, B_PART:B_PART + 4, :].rearrange("p b (m r) -> p (b m) r", r=P).rearrange(
                                      "p (c m) r -> p c m r", c=2), AX.X, ALU.add).then_inc(part_read, 1)

            def norm(s):
                dve.wait_ge(stats_made.sem, stats_made.after(s))
                dve.tensor_scalar(msq[:, 0:TT], ps[:, B_NORM, 0:TT], 1.0 / D, RMS_EPS, ALU.mult,
                                  ALU.add).then_inc(ms_ready.sem, 1)
                dve.wait_ge(rstd_ready.sem, rstd_ready.after(s))
                dve.tensor_tensor(diag[:], ident[:].unsqueeze(1).to_broadcast([P, TT, P]),
                                  rstd[:, 0:TT].unsqueeze(2).to_broadcast([P, TT, P]),
                                  ALU.mult).then_inc(diag_ready.sem, 1)
                dve.wait_ge(rbc_made.sem, rbc_made.after(s))
                m = mod[:, 3 * KD * (s % 3):3 * KD * (s % 3 + 1), :]

                def low(k):
                    dve.wait_ge(h_hi_ready.sem, h_hi_ready.after(s, k))
                    for c, (i, j) in enumerate(((0, P), (P, N_TOK))):
                        ins = dve.scalar_tensor_tensor(out=h_lo[:, k, i:j], in0=tmp[k % 2][:, i:j],
                                                       scalar=m[:, k, c:c + 1], in1=h_hi[:, k, i:j],
                                                       op0=ALU.add, op1=ALU.subtract)
                    ins.then_inc(h_ready.sem, 1)

                for k in range(KD):
                    if k >= 2:
                        low(k - 2)
                        dve.wait_ge(h_ready.sem, h_ready.after(s, k - 2))
                    for c, (i, j) in enumerate(((0, P), (P, N_TOK))):
                        ins = dve.scalar_tensor_tensor(out=tmp[k % 2][:, i:j], in0=x[:, k, i:j],
                                                       scalar=m[:, KD + k, c:c + 1], in1=ps[:, B_NORM, i:j],
                                                       op0=ALU.mult, op1=ALU.mult)
                    ins.then_inc(xr_ready.sem, 1)
                low(KD - 2)
                low(KD - 1)

            def add_squares(s, m, par):
                dve.wait_ge(sq_ready.sem, sq_ready.after(s, m))
                dve.wait_ge(ssq_ready.sem, ssq_ready.at[s] + m)
                dve.tensor_tensor(ssq[:], ssq[:], sq[par][:], ALU.add).then_inc(ssq_ready.sem, 1)

            def residual(s, m, bank, done, val):
                dve.wait_ge(done, val)
                g = mod[:, 3 * KD * (s % 3):3 * KD * (s % 3 + 1), :]
                for c, (i, j) in enumerate(((0, P), (P, N_TOK))):
                    if isinstance(m, int):
                        xs, gate = x[:, m, i:j], g[:, 2 * KD + m, c:c + 1]
                    else:
                        xs = x[:, bass.ds(m, 1), i:j].rearrange("p o t -> p (o t)")
                        gate = g[:, bass.ds(2 * KD + m, 1), c:c + 1].rearrange("p o c -> p (o c)")
                    ins = dve.scalar_tensor_tensor(out=xs, in0=ps[:, bank, i:j], scalar=gate, in1=xs,
                                                   op0=ALU.mult, op1=ALU.add)
                ins.then_inc(x_updated.sem, 1)

            def gu_step(s, j, par, w_next, part=None, slabs=()):
                def sum_next(ks):
                    for k in ks:
                        dve.wait_ge(slab_scaled, scaled_to(part, k))
                        sum_slab(part, k, slab[k % SLAB_SLOTS], acc)

                split_lo(CB[s] + j + 1 - (1 - par), 1 - par, w_next)
                sum_next(slabs[0:2])
                dve.wait_ge(silu_ready.sem, silu_ready.after(s, j))
                dve.wait_ge(act_ready.sem, act_ready.at[s] + j - 1)
                dve.tensor_tensor(prod[par][:], ps[:, 2 * par + 1, 0:N_TOK], sil[par][:],
                                  ALU.mult).then_inc(prod_ready.sem, 1)
                dve.wait_ge(act_hi_ready.sem, act_hi_ready.after(s, j))
                cols = bass.ds(j * N_TOK, N_TOK)
                dve.tensor_tensor(act_lo[:, cols], prod[par][:], act_hi[:, cols],
                                  ALU.subtract).then_inc(act_ready.sem, 1)
                sum_next(slabs[2:])

            def dn_step(s, m, par, w_next):
                if w_next:
                    split_lo(CB[s] + GU_STEPS + m + 1 - (1 - par), 1 - par, w_next)
                residual(s, m, par, w_used.sem, w_used.after(s, GU_STEPS + m))
                add_squares(s, m, par)

            def clear_squares(s):
                dve.wait_ge(rbc_made.sem, rbc_made.after(s))
                chain.link(dve.memset(ssq[:], 0.0))

            def mixer_constants(s):
                kind = stage_kind(s)
                v = tiles[kind]
                dve.wait_ge(mixer_in, n_loads[kind])
                if kind in "AB":
                    nh = HPG[kind] + KVPG[kind]
                    g4 = v["g"].rearrange("p (h e two) -> p h e two", h=nh, two=2)
                    for t in range(2):
                        cos = v["cos"][:, t, :].unsqueeze(1).to_broadcast([P, nh, HD])
                        chain.link(dve.tensor_tensor(v["cg"][:, t, :].rearrange("p (h d) -> p h d", h=nh),
                                                     v["g"].rearrange("p (h d) -> p h d", h=nh), cos, ALU.mult))
                        for e in range(2):
                            sg = v["sg"][:, t, :].rearrange("p (h e two) -> p h e two", h=nh, two=2)[:, :, :, e]
                            sin = v["sin"][:, t, :].rearrange("p (e two) -> p e two", two=2)[:, :, e]
                            chain.link(dve.tensor_tensor(sg, g4[:, :, :, 1 - e],
                                                         sin.unsqueeze(1).to_broadcast([P, nh, HD // 2]), ALU.mult))
                if kind == "A":
                    chain.link(dve.tensor_scalar(v["sink8"][:], v["sink"][:], 1 / scale_of["A"], None, ALU.mult))

            def head_norm(s, g):
                kind = stage_kind(s)
                v = tiles[kind]
                dve.wait_ge(rsq_ready.sem, rsq_ready.after((s, g)))
                if kind == "C":
                    regions = ((slice(0, TT), slice(0, 2), 6, 0), (slice(0, 4), slice(2, 4), 8, 6))
                    for t, h, n, at in regions:
                        chain.link(dve.tensor_reduce(v["hms"][:, at:at + n].rearrange("p (t h) -> p t h", h=2),
                                                     v["sqc"][:, t, h, :], AX.X, ALU.add))
                    dve.tensor_scalar(v["hms"][:, 0:14], v["hms"][:, 0:14], 1.0 / C_QK, RMS_EPS, ALU.mult,
                                      ALU.add).then_inc(hms_ready.sem, 1)
                    yield
                    yield
                    yield
                    yield
                    dve.wait_ge(head_scaled.sem, head_scaled.after((s, g)))
                    for t in (1, 2):
                        z = v["cat"][g % 2][:, t, :, C_NOPE:C_QK]
                        z2 = z.rearrange("p h (e two) -> p h e two", two=2)
                        r = v["rope"][:, t - 1]
                        r2 = r.rearrange("p h (e two) -> p h e two", two=2)
                        sin = v["sin"][:, t - 1, :].rearrange("p (e two) -> p e two", two=2)
                        for e in range(2):
                            dve.tensor_tensor(r2[:, :, :, e], z2[:, :, :, 1 - e],
                                              sin[:, :, e].unsqueeze(1).to_broadcast([P, 4, C_ROPE // 2]),
                                              ALU.mult).then_inc(dve_step, 1)
                            chain.local += 1
                        dve.wait_ge(dve_step, chain.value())
                        chain.link(dve.tensor_tensor(z, z, v["cos"][:, t - 1, :].unsqueeze(1).to_broadcast(
                            [P, 4, C_ROPE]), ALU.mult))
                        ins = dve.tensor_tensor(z, z, r, ALU.add)
                        if t == 1:
                            chain.link(ins)
                        else:
                            ins.then_inc(qn_ready.sem, 1)
                        yield
                    return
                nh = HPG[kind] + KVPG[kind]
                hms = v["hms"][:, 0:TT * nh]
                nrm = v["nrm"].rearrange("p t (h d) -> p t h d", h=nh)
                chain.link(dve.tensor_reduce(hms.rearrange("p (t h) -> p t h", h=nh), nrm, AX.X, ALU.add))
                dve.tensor_scalar(hms, hms, 1.0 / HD, RMS_EPS, ALU.mult, ALU.add).then_inc(hms_ready.sem, 1)
                yield
                yield
                yield
                dve.wait_ge(head_scaled.sem, head_scaled.after((s, g)))
                if g >= 1:
                    dve.wait_ge(kv_out, kv_sent[s, g - 1])
                qn = v["qn"]
                if kind == "D":
                    dve.tensor_tensor(qn[:], v["nrm"][:], v["g"][:].unsqueeze(1).to_broadcast([P, TT, nh * HD]),
                                      ALU.mult).then_inc(qn_ready.sem, 1)
                    yield
                    return
                chain.link(dve.tensor_tensor(qn[:, 0, 0:nh * HD], v["nrm"][:, 0, :], v["g"][:], ALU.mult))
                lat = v["nrm"][:, 1:3, :]
                pair = "p t (e two) -> p t e two"
                for e in range(2):
                    chain.link(dve.tensor_tensor(v["rope"].rearrange(pair, two=2)[:, :, :, e],
                                                 lat.rearrange(pair, two=2)[:, :, :, 1 - e],
                                                 v["sg"].rearrange(pair, two=2)[:, :, :, e], ALU.mult))
                yield
                chain.link(dve.tensor_tensor(lat, lat, v["cg"][:], ALU.mult))
                yield
                chain.link(dve.tensor_tensor(qn[:, 1:3, 0:nh * HD], lat, v["rope"][:], ALU.add))
                dve.tensor_copy(qn[:, :, nh * HD:(nh + 1) * HD], qn[:, :, (nh - 1) * HD:nh * HD]
                                ).then_inc(qn_ready.sem, 1)
                yield

            def head_bias(s, g):
                v = tiles["D"]
                dve.wait_ge(bias_in[g % 2], 64 * (g // 2 + 1))
                b = v["bias"][g % 2].rearrange("p h d c -> p (h d) c")
                chain.link(dve.scalar_tensor_tensor(out=b, in0=b, scalar=1 / scale_of["D"],
                                                    in1=v["mask"][:].unsqueeze(1).to_broadcast([P, 12, GRID_W]),
                                                    op0=ALU.mult, op1=ALU.add))

            def maximum(s, g, u, uu):
                kind = stage_kind(s)
                v = tiles[kind]
                what, h, t = units(kind)[u]
                bank, st = B_S[uu % 2], v["stat"]
                dve.wait_ge(s_made.sem, s_made.after((s, g, u)))
                n = HPG[kind] if what == "ctx" else 1
                w = P if what == "ctx" else N_LAT + N_PAST
                if kind == "A" and what == "lat":
                    blk = ps[:, bank, (2 - t) * P:(3 - t) * P]
                    chain.link(dve.tensor_tensor(blk, blk, v["mask"][:, t - 1, :], ALU.add))
                if kind == "D" and what == "lat":
                    blk = ps[:, bank, 0:N_LAT].rearrange("p (r c) -> p r c", c=GRID_W)
                    d0 = 4 - 2 * t
                    b = v["bias"][g % 2][:, h, d0:d0 + GRID_H, :]
                    rev = bass.AP(tensor=b.tensor, offset=b.offset + GRID_W - 1,
                                  ap=[list(b.ap[0]), [GRID_W, GRID_H], [-1, GRID_W]])
                    chain.link(dve.tensor_tensor(blk, blk, rev, ALU.add))
                chain.link(dve.tensor_reduce(st[:, uu % 3, 0, 0:n],
                                             ps[:, bank, 0:n * w].rearrange("p (n w) -> p n w", w=w), AX.X, ALU.max))
                mx, nb = st[:, uu % 3, 0, 0:n], st[:, uu % 3, 1, 0:n]
                if kind != "A":
                    dve.tensor_scalar(nb, mx, -scale_of[kind], None, ALU.mult).then_inc(max_ready.sem, 1)
                    return
                h0 = g * HPG[kind] + (0 if what == "ctx" else h)
                chain.link(dve.tensor_tensor(mx, mx, v["sink8"][:, h0:h0 + n], ALU.max))
                chain.link(dve.tensor_scalar(nb, mx, -scale_of[kind], None, ALU.mult))
                dve.tensor_tensor(st[:, uu % 3, 3, 0:n], v["sink"][:, h0:h0 + n], nb, ALU.add
                                  ).then_inc(max_ready.sem, 1)

            def inverse(s, g, u, uu):
                kind = stage_kind(s)
                v = tiles[kind]
                what, h, t = units(kind)[u]
                st = v["stat"][:, uu % 3]
                n = HPG[kind] if what == "ctx" else 1
                dve.wait_ge(exp_ready.sem, exp_ready.after((s, g, u)))
                if kind == "A":
                    chain.link(dve.tensor_tensor(st[:, 2, 0:n], st[:, 2, 0:n], st[:, 3, 0:n], ALU.add))
                r = v["rinv"][:, uu % 4, 0:n]
                chain.link(dve.reciprocal(r, st[:, 2, 0:n]))
                if n == 1:
                    p = v["p"][uu % 3][:, 0:N_LAT + N_PAST]
                    ins = dve.tensor_scalar(p, p, r, None, ALU.mult)
                else:
                    p = v["p"][uu % 3][:, 0:n * P].rearrange("p (n w) -> p n w", n=n)
                    ins = dve.tensor_tensor(p, p, r.unsqueeze(2).to_broadcast([P, n, P]), ALU.mult)
                ins.then_inc(p_scaled.sem, 1)

            def o_lo(s, g):
                kind = stage_kind(s)
                v = tiles[kind]
                dve.wait_ge(ot_hi_ready.sem, ot_hi_ready.after((s, g)))
                for n in range(HPG[kind] // 2):
                    k = g * HPG[kind] // 2 + n
                    ins = dve.tensor_tensor(v["oT_lo"][:, k, :], ps[:, out_bank(kind, g, n), 0:N_TOK], v["oT_hi"][:, k, :],
                                            ALU.subtract)
                ins.then_inc(ot_ready.sem, 1)

            def compress(s):
                v = tiles["C"]
                split_lo(CB[s], 1, width(s, 1))
                split_lo(CB[s] + 2, 0, width(s, 2))
                dve.wait_ge(c_raw_ready, 1)
                for c, n in enumerate((C_Q_RANK, C_KV_RANK)):
                    ins = dve.tensor_scalar(v["cms"][:, c, :], v["cms"][:, c, :], 1.0 / n, RMS_EPS, ALU.mult, ALU.add)
                    if c == 0:
                        chain.link(ins)
                ins.then_inc(c_norm_ready.sem, 1)
                dve.tensor_copy(v["kr"][:, 0:TT, :], v["cdn"][:, :, C_Q_RANK + C_KV_RANK:C_DOWN]
                                ).then_inc(c_norm_ready.sem, 1)
                dve.wait_ge(c_rstd_ready.sem, 1)
                for c, (i, j) in enumerate(((0, C_Q_RANK), (C_Q_RANK, C_Q_RANK + C_KV_RANK))):
                    for t in range(TT):
                        ins = dve.scalar_tensor_tensor(out=v["cdn"][:, t, i:j], in0=v["cdn"][:, t, i:j],
                                                       scalar=v["crs"][:, c, t:t + 1], in1=v["gd"][:, i:j],
                                                       op0=ALU.mult, op1=ALU.mult)
                ins.then_inc(c_norm_ready.sem, 1)
                for n in range(KQ + KC):
                    dve.wait_ge(c_hi_ready, n + 1)
                    hi, lo = ((v["cqT_hi"][:, n, :], v["cqT_lo"][:, n, :]) if n < KQ else
                              (v["ckT_hi"][:, n - KQ, 0:N_TOK], v["ckT_lo"][:, n - KQ, 0:N_TOK]))
                    dve.tensor_tensor(lo, ps[:, CT_BANKS[n], 0:N_TOK], hi, ALU.subtract).then_inc(c_t_ready, 1)
                dve.wait_ge(c_hi_ready, KQ + KC + 1)
                dve.tensor_tensor(v["ckT_lo"][:, :, N_TOK:N_TOK + N_PAST], v["cache"][:],
                                  v["ckT_hi"][:, :, N_TOK:N_TOK + N_PAST], ALU.subtract).then_inc(c_t_ready, 1)

            chain.link(dve.memset(ssq[:], 0.0))
            dve.wait_ge(act_step, 1)
            for part in range(3):
                for k in range(KD):
                    n = part * KD + k
                    batch = n // BOOT_BATCH
                    dve.wait_ge(boot_landed[batch % BOOT_SLOTS], 16 * (batch // BOOT_SLOTS + 1))
                    sum_slab(part, k, boot[batch % BOOT_SLOTS][:, n % BOOT_BATCH, :],
                             acc_of_scale if part == 1 else acc, (0, 1) if part == 0 else (1,))
                if part == 1:
                    sum_partitions(0, 0)
            dve.wait_ge(consts_in, 16 * 3)
            for m in range(KD):
                add_squares(-1, m, m % 2)
            sum_partitions(1, 1)
            sum_partitions(2, 2)
            dve.wait_ge(part_read, 3)
            modulation(0, 3)
            split_lo(0, 0, GU_CHUNK)
            uu = 0
            for s in range(N_STAGE):
                norm(s)
                clear_squares(s)
                kind = stage_kind(s)
                if kind == "F":
                    part, n, at = first_part(s), n_parts(s), first_part(s) % N_PART
                    for q in range(4):
                        gu_step(s, q, q % 2, GU_CHUNK, part, SLABS[q])
                    sum_partitions(part, at)
                    if n > 1:
                        with dve.Fori(1, n) as i:
                            for q in range(4):
                                gu_step(s, 4 * i + q, q % 2, GU_CHUNK, part + i, SLABS[q])
                            sum_partitions(part + i, i + 3 if at == 3 else i - 1)
                    if 2 * n < (GU_STEPS - 2) // 2:
                        with dve.Fori(2 * n, (GU_STEPS - 2) // 2) as pair:
                            i = 2 * pair
                            for par in range(2):
                                gu_step(s, i + par, par, GU_CHUNK)
                    gu_step(s, GU_STEPS - 2, 0, GU_CHUNK)
                    gu_step(s, GU_STEPS - 1, 1, DN_CHUNK)
                    dve.wait_ge(part_read, part + n)
                    if at == 3:
                        modulation(part, n)
                    else:
                        modulation(part, 1)
                        if n > 1:
                            modulation(part + 1, n - 1)
                    with dve.Fori(0, (DN_STEPS - 2) // 2) as pair:
                        i = 2 * pair
                        for par in range(2):
                            dn_step(s, i + par, par, DN_CHUNK)
                    dn_step(s, DN_STEPS - 2, 0, DN_CHUNK)
                    dn_step(s, DN_STEPS - 1, 1, width(s, GU_STEPS + DN_STEPS))
                    continue
                n_g, n_u, nd = GROUPS[kind], len(units(kind)), n_down[kind]

                def split_chunk(c):
                    if width(s, c):
                        split_lo(CB[s] + c - c % 2, c % 2, width(s, c))

                mixer_constants(s)
                if kind == "C":
                    compress(s)
                split_chunk(nd + 1)
                for i, _ in enumerate(head_norm(s, 0)):
                    if i == 0:
                        split_chunk(nd + 2)
                for g in range(n_g):
                    more = g + 2 < n_g
                    ahead = head_norm(s, g + 1) if g + 1 < n_g else iter(())
                    if kind == "D":
                        head_bias(s, g)
                    for u in range(n_u + 3):
                        if u == n_u + 1:
                            for _ in ahead:
                                pass
                        if u < n_u:
                            maximum(s, g, u, uu + u)
                        if u == 1 and g >= 1:
                            o_lo(s, g - 1)
                        if 1 <= u <= n_u:
                            inverse(s, g, u - 1, uu + u - 1)
                        if u == 2 and more:
                            split_chunk(nd + g + 3)
                        next(ahead, None)
                    uu += n_u
                o_lo(s, n_g - 1)
                for c in range(WO_STEPS):
                    split_chunk(nd + n_g + c + 1)
                    for b in range(2):
                        m = 2 * c + b
                        if b == 0:
                            residual(s, m, b, wo_half.sem, wo_half.after(s, c))
                        else:
                            residual(s, m, b, w_used.sem, w_used.after(s, nd + n_g + c))
                        add_squares(s, m, b)


def kernel(**inputs):
    import concourse.bacc as bacc
    from concourse.bass_utils import run_bass_kernel_spmd

    def arr(name):
        return np.asarray(inputs[name])

    def rows(w, *shape):
        return w.reshape(w.shape[0] // P, P, *shape)

    def by_channel(w):
        return w.reshape(w.shape[0], -1, P).transpose(2, 0, 1)

    a = {}
    x = np.concatenate([arr("x_prompt")[0], arr("x_sample")[0]], axis=0)
    a["x"] = x.T.reshape(KD, P, N_TOK).transpose(1, 0, 2)
    a["cond"] = np.stack([arr("c_ctx"), arr("c")[0]], axis=-1).reshape(KD, P, 2).transpose(1, 0, 2)
    a["mod_w"] = arr("mod_w").reshape(DEPTH, KD, P, N_PART, D).transpose(0, 3, 1, 2, 4).reshape(-1, P, D)
    a["mod_b"] = arr("mod_b").reshape(-1, P).T
    a["gains"] = by_channel(np.stack([arr("norm_ff1"), arr("norm_mix"), arr("norm_ff2")], axis=1).reshape(N_STAGE, D))
    a["ident"] = np.eye(P, dtype=np.float32)
    gu = np.stack([arr("ff1_w_gu"), arr("ff2_w_gu")], axis=1)
    a["ffn_gu"] = gu.reshape(2 * DEPTH, KD, P, 2, KF, P).transpose(0, 4, 2, 1, 3, 5).reshape(-1, P, GU_CHUNK)
    dn = np.stack([arr("ff1_w_down"), arr("ff2_w_down")], axis=1)
    a["ffn_dn"] = dn.reshape(2 * DEPTH, KF, P, KD, P).transpose(0, 3, 2, 1, 4).reshape(-1, P, DN_CHUNK)

    def wo(w):
        return w.reshape(KD, P, WO_STEPS, 2 * P).transpose(2, 1, 0, 3).reshape(WO_STEPS, P, WO_CHUNK)

    def qkv(w, heads, kv_heads, groups):
        w = w.reshape(KD, P, -1)
        nq, nk = heads * HD, kv_heads * HD
        parts = [w[:, :, i:i + n].reshape(KD, P, groups, n // groups)
                 for i, n in ((0, nq), (nq, nk), (nq + nk, nk))]
        return np.concatenate(parts, axis=3).transpose(2, 1, 0, 3).reshape(groups, P, QKV_CHUNK)

    pos = np.arange(N_LAT)

    def rope(dim):
        n = dim // 4
        inv = np.float32(ROPE_THETA) ** (-np.arange(n, dtype=np.float32) / np.float32(n))
        ang = np.concatenate([(pos // GRID_W).astype(np.float32)[:, None] * inv,
                              (pos % GRID_W).astype(np.float32)[:, None] * inv], axis=-1)
        c, s = np.cos(ang), np.sin(ang)
        c, s = np.stack([c, c], axis=-1), np.stack([-s, s], axis=-1)
        return [z.reshape(2, P, dim).transpose(1, 0, 2) for z in (c, s)]

    def everywhere(v):
        return np.broadcast_to(v, (P, *v.shape))

    for kind in "ab":
        a[f"{kind}_w"] = qkv(arr(f"{kind}_w_qkv")[0], HEADS, KV_HEADS, 4)
        a[f"{kind}_wo"] = wo(arr(f"{kind}_w_o")[0])
        a[f"{kind}_g"] = everywhere(np.concatenate([arr(f"{kind}_q_norm")[0]] * 4 + [arr(f"{kind}_k_norm")[0]]))
        a[f"{kind}_cos"], a[f"{kind}_sin"] = rope(HD)
        ck = arr(f"cache_{kind}_k")[0, 0].transpose(2, 1, 0)
        a[f"{kind}_ck"] = np.concatenate([ck, ck], axis=0)
        a[f"{kind}_cv"] = arr(f"cache_{kind}_v")[0, 0].reshape(N_PAST, KV_HEADS * HD)
    q, k = pos[:, None], pos[None, :]
    outside = np.where(np.abs(q - k) <= A_WINDOW, np.float32(0), np.float32(NEG))
    a["a_mask"] = np.stack([outside[0:P, P:], outside[P:, 0:P]], axis=1)
    a["a_sink"] = everywhere(arr("a_sink")[0])

    dn = arr("c_w_down")[0].reshape(KD, P, C_DOWN).transpose(1, 0, 2)
    a["c_dn0"] = dn[:, :, 0:C_Q_RANK].reshape(P, -1)
    a["c_dn1"] = dn[:, :, C_Q_RANK:].reshape(P, -1)
    uq = arr("c_w_uq")[0].reshape(KQ, P, 8, C_UQ_W).transpose(2, 1, 0, 3).reshape(8, P, -1)
    ukv = arr("c_w_ukv")[0].reshape(KC, P, 8, C_UKV_W).transpose(2, 1, 0, 3).reshape(8, P, -1)
    a["c_w"] = np.concatenate([uq, ukv], axis=2)
    a["c_wo"] = wo(arr("c_w_o")[0])
    a["c_g"] = everywhere(np.stack([arr("c_q_norm")[0], arr("c_k_norm")[0]]))
    a["c_gd"] = everywhere(np.concatenate([arr("c_q_lnorm")[0], arr("c_kv_lnorm")[0]]))
    a["c_cos"], a["c_sin"] = rope(C_ROPE)
    a["c_cache"] = arr("cache_c_kv")[0, 0].T.reshape(KC, P, N_PAST).transpose(1, 0, 2)
    a["c_kr"] = arr("cache_c_krope")[0, 0]

    a["d_w"] = qkv(arr("d_w_qkv")[0], HEADS, HEADS, 8)
    a["d_wo"] = wo(arr("d_w_o")[0])
    a["d_g"] = everywhere(np.concatenate([arr("d_q_norm")[0]] * 2 + [arr("d_k_norm")[0]] * 2))
    a["d_ck"] = arr("cache_d_k")[0, 0].transpose(1, 2, 0).reshape(8, P, N_PAST).transpose(1, 0, 2)
    a["d_cv"] = arr("cache_d_v")[0, 0].reshape(N_PAST, HEADS * HD)
    rpb = np.zeros((HEADS, RPB_R, RPB_W), np.float32)
    rpb[:, :, RPB_PAD:RPB_PAD + RPB_C] = arr("d_rpb")[0, :, :, ::-1]
    a["d_rpb"] = rpb
    qc, kc = np.arange(GRID_W)[:, None], np.arange(GRID_W)[None, ::-1]
    first = np.clip(qc - NA_COLS // 2, 0, GRID_W - NA_COLS)
    inside = np.where((kc >= first) & (kc < first + NA_COLS), np.float32(0), np.float32(NEG))
    a["d_mask"] = np.concatenate([inside, inside], axis=0)

    outs = {"y": (P, KD, N_TOK), "new_a_k": (P, KV_HEADS * HD), "new_a_v": (P, KV_HEADS * HD),
            "new_b_k": (P, KV_HEADS * HD), "new_b_v": (P, KV_HEADS * HD),
            "new_c_kv": (P, C_KV_RANK), "new_c_krope": (P, C_ROPE),
            "new_d_k": (P, HEADS * HD), "new_d_v": (P, HEADS * HD)}
    nc = bacc.Bacc("TRN2", target_bir_lowering=False, num_devices=1)
    arrays, ins = {}, {}
    for name, v in a.items():
        v = np.ascontiguousarray(v)
        arrays[f"in_{name}"] = v
        ins[name] = nc.dram_tensor(f"in_{name}", v.shape, F32, kind="ExternalInput").ap()
    outputs = {name: nc.dram_tensor(f"out_{name}", shape, F32, kind="ExternalOutput").ap()
               for name, shape in outs.items()}
    build(nc, ins, outputs)
    got = run_bass_kernel_spmd(nc, [arrays], core_ids=[0]).results[0]
    r = {name: np.asarray(got[f"out_{name}"]) for name in outs}
    y = r["y"].transpose(1, 0, 2).reshape(D, N_TOK).T
    return (y[0:N_CTX][None], y[N_CTX:][None],
            r["new_a_k"].reshape(1, 1, P, KV_HEADS, HD), r["new_a_v"].reshape(1, 1, P, KV_HEADS, HD),
            r["new_b_k"].reshape(1, 1, P, KV_HEADS, HD), r["new_b_v"].reshape(1, 1, P, KV_HEADS, HD),
            r["new_c_kv"].reshape(1, 1, P, C_KV_RANK), r["new_c_krope"].reshape(1, 1, P, C_ROPE),
            r["new_d_k"].reshape(1, 1, P, HEADS, HD), r["new_d_v"].reshape(1, 1, P, HEADS, HD))
```
